# Optimizing a Trainium2 kernel written in Bass

```python
import math
import jax
import jax.numpy as jnp
from jax import lax
import numpy as np

D_MODEL = 1024
BATCH = 1
SEQ = 256
DEPTH = 2

GRID_W = 64
CTX_LEN = 256
N_MIXERS = 2
N_SSM_LAYERS = (DEPTH + 1) // 2
N_CONV_LAYERS = DEPTH // 2

D_INNER = 2 * D_MODEL
SSM_HEADDIM = 64
SSM_HEADS = D_INNER // SSM_HEADDIM
SSM_GROUPS = 8
HEADS_PER_GROUP = SSM_HEADS // SSM_GROUPS
D_STATE = 128
SSM_CONV = 5
CHUNK = 128
CONV_DIM = D_INNER + 2 * SSM_GROUPS * D_STATE
D_IN_PROJ = D_INNER + CONV_DIM + 2 * SSM_HEADS

CONF_WIDTH = 31

N_EXPERTS = 64
TOP_K = 8
N_EXPERT_GROUPS = 8
TOPK_GROUPS = 4
D_EXPERT = 256
D_SHARED = 256
ROUTED_SCALE = 2.5
MOE_BLOCK = 128

EPS = 1e-6

kernel_name = 'hybrid_ssd_conformer_moe_dit'

def rms_norm(x, g):
    x32 = x.astype(jnp.float32)
    y = x32 * lax.rsqrt(jnp.mean(x32 * x32, axis=-1, keepdims=True) + EPS)
    return (y * g.astype(jnp.float32)).astype(x.dtype)

def layer_norm(x, g, b):
    x32 = x.astype(jnp.float32)
    mu = jnp.mean(x32, axis=-1, keepdims=True)
    xc = x32 - mu
    y = xc * lax.rsqrt(jnp.mean(xc * xc, axis=-1, keepdims=True) + EPS)
    return (y * g.astype(jnp.float32) + b.astype(jnp.float32)).astype(x.dtype)

def dwconv(x, w, b):
    k, ch = w.shape
    y = lax.conv_general_dilated(x.astype(w.dtype), w[:, None, :], window_strides=(1,),
                                 padding=[(k // 2, k // 2)],
                                 dimension_numbers=('NWC', 'WIO', 'NWC'),
                                 feature_group_count=ch)
    return y + b

def ssd_scan(x, dt, a, b, c, h0):
    bsz, L, G, R, P = x.shape
    N = b.shape[-1]
    nc = L // CHUNK
    xdt = (x * dt[..., None]).reshape(bsz, nc, CHUNK, G, R, P)
    bq = b.reshape(bsz, nc, CHUNK, G, N)
    cq = c.reshape(bsz, nc, CHUNK, G, N)
    cs = jnp.cumsum((dt * a).reshape(bsz, nc, CHUNK, G, R), axis=2)
    tri = jnp.tril(jnp.ones((CHUNK, CHUNK), dtype=bool))[None, None, :, :, None, None]
    decay = jnp.exp(jnp.where(tri, cs[:, :, :, None] - cs[:, :, None, :], -jnp.inf))
    cb = jnp.einsum('bclgn,bcsgn->bclsg', cq, bq)
    y_diag = jnp.einsum('bclsgr,bcsgrp->bclgrp', cb[..., None] * decay, xdt)
    w_end = jnp.exp(cs[:, :, -1:] - cs)
    states = jnp.einsum('bcsgn,bcsgrp->bcgrpn', bq, xdt * w_end[..., None])
    chunk_decay = jnp.exp(cs[:, :, -1])

    def step(h, inp):
        st, dec = inp
        return h * dec[..., None, None] + st, h

    h_last, h_start = lax.scan(step, h0, (jnp.moveaxis(states, 1, 0), jnp.moveaxis(chunk_decay, 1, 0)))
    h_start = jnp.moveaxis(h_start, 0, 1)
    y_off = jnp.einsum('bclgn,bcgrpn->bclgrp', cq, h_start) * jnp.exp(cs)[..., None]
    return (y_diag + y_off).reshape(bsz, L, G, R, P), h_last

def mamba_mixer(h_lat, h_ctx, w_in, conv_w, conv_b, dt_bias, a_log, d_skip, norm_w, w_out, ctx_out):
    G, R, P, N = SSM_GROUPS, HEADS_PER_GROUP, SSM_HEADDIM, D_STATE
    a = -jnp.exp(a_log.astype(jnp.float32)).reshape(2, G, R)
    dtb = dt_bias.astype(jnp.float32).reshape(2, G, R)

    def project(h):
        bsz, L, _ = h.shape
        z, xbc, dtr = jnp.split(h @ w_in, [D_INNER, D_INNER + CONV_DIM], axis=-1)
        xbc = jax.nn.silu(dwconv(xbc, conv_w, conv_b))
        xs, bs, cs = jnp.split(xbc, [D_INNER, D_INNER + G * N], axis=-1)
        dt = jax.nn.softplus(dtr.astype(jnp.float32).reshape(bsz, L, 2, G, R) + dtb)
        return (z, xs.reshape(bsz, L, G, R, P), bs.reshape(bsz, L, G, N),
                cs.reshape(bsz, L, G, N), dt)

    def flip(t):
        return jnp.flip(t, axis=1)

    def output(z, xs, y_fwd, y_bwd_rev):
        bsz, L = z.shape[:2]
        y = y_fwd + flip(y_bwd_rev) + xs * d_skip.reshape(G, R, 1)
        y = y.reshape(bsz, L, D_INNER) * jax.nn.silu(z.astype(jnp.float32))
        yg = y.reshape(bsz, L, G, D_INNER // G)
        yg = yg * lax.rsqrt(jnp.mean(yg * yg, axis=-1, keepdims=True) + EPS)
        y = yg.reshape(bsz, L, D_INNER) * norm_w
        return y.astype(w_out.dtype) @ w_out

    zc, xc, bc, cc, dtc = project(h_ctx)
    zl, xl, bl, cl, dtl = project(h_lat)
    h0 = jnp.zeros((h_lat.shape[0], G, R, P, N), jnp.float32)
    yc_f, st_f = ssd_scan(xc, dtc[:, :, 0], a[0], bc, cc, h0)
    yc_b, st_b = ssd_scan(flip(xc), flip(dtc[:, :, 1]), a[1], flip(bc), flip(cc), h0)
    yl_f, _ = ssd_scan(xl, dtl[:, :, 0], a[0], bl, cl, st_f)
    yl_b, _ = ssd_scan(flip(xl), flip(dtl[:, :, 1]), a[1], flip(bl), flip(cl), st_b)
    y_lat = output(zl, xl, yl_f, yl_b)
    y_ctx = output(zc, xc, yc_f, yc_b) if ctx_out else None
    return y_lat, y_ctx

def conformer_mixer(h, n_rows, row_len, w_in, b_in, dw_w, dw_b, ln_g, ln_b, w_out, b_out):
    bsz, L, d = h.shape
    u = h @ w_in + b_in
    u = u[..., :d] * jax.nn.sigmoid(u[..., d:])
    u = dwconv(u.reshape(bsz * n_rows, row_len, d), dw_w, dw_b).reshape(bsz, L, d)
    u = jax.nn.silu(layer_norm(u, ln_g, ln_b))
    return u @ w_out + b_out

def moe_ffn(h, router_w, router_b, w_gate, w_up, w_down, s_gate, s_up, s_down):
    T, d = h.shape
    scores = jax.nn.sigmoid(h.astype(jnp.float32) @ router_w.astype(jnp.float32))
    sel = scores + router_b.astype(jnp.float32)
    grp_score = lax.top_k(sel.reshape(T, N_EXPERT_GROUPS, -1), 2)[0].sum(-1)
    _, gidx = lax.top_k(grp_score, TOPK_GROUPS)
    gmask = jnp.zeros((T, N_EXPERT_GROUPS), bool).at[jnp.arange(T)[:, None], gidx].set(True)
    emask = jnp.repeat(gmask, N_EXPERTS // N_EXPERT_GROUPS, axis=1)
    _, eidx = lax.top_k(jnp.where(emask, sel, -jnp.inf), TOP_K)
    gate = jnp.take_along_axis(scores, eidx, axis=1)
    gate = gate / jnp.sum(gate, axis=-1, keepdims=True) * ROUTED_SCALE

    A = T * TOP_K
    flat_e = eidx.reshape(A)
    order = jnp.argsort(flat_e)
    sorted_e = flat_e[order]
    tok = (order // TOP_K).astype(jnp.int32)
    wts = gate.reshape(A)[order]
    counts = jnp.bincount(flat_e, length=N_EXPERTS)
    start = jnp.cumsum(counts) - counts
    padded = (counts + MOE_BLOCK - 1) // MOE_BLOCK * MOE_BLOCK
    pend = jnp.cumsum(padded)
    dest = (pend - padded)[sorted_e] + jnp.arange(A) - start[sorted_e]
    n_blocks = -(-(A + N_EXPERTS * (MOE_BLOCK - 1)) // MOE_BLOCK)
    P = n_blocks * MOE_BLOCK
    row_tok = jnp.zeros((P,), jnp.int32).at[dest].set(tok)
    row_w = jnp.zeros((P,), jnp.float32).at[dest].set(wts)
    block_e = jnp.minimum(jnp.searchsorted(pend, jnp.arange(n_blocks) * MOE_BLOCK, side='right'),
                          N_EXPERTS - 1)

    def expert_block(args):
        rows, e = args
        xb = h[rows]
        return (jax.nn.silu(xb @ w_gate[e]) * (xb @ w_up[e])) @ w_down[e]

    yb = lax.map(expert_block, (row_tok.reshape(n_blocks, MOE_BLOCK), block_e))
    routed = jnp.zeros((T, d), jnp.float32).at[row_tok].add(yb.reshape(P, d).astype(jnp.float32) * row_w[:, None])
    shared = (jax.nn.silu(h @ s_gate) * (h @ s_up)) @ s_down
    return (routed + shared).astype(h.dtype)

def setup_inputs(seed: int = 0) -> dict:
    key = jax.random.key(seed)
    k = jax.random.split(key, 40)
    f32 = jnp.float32

    def nrm(i, shape, scale):
        return jax.random.normal(k[i], shape, f32) * scale

    def gain(i, shape):
        return 1.0 + nrm(i, shape, 0.05)

    D, NS, NC, E = D_MODEL, N_SSM_LAYERS, N_CONV_LAYERS, N_EXPERTS
    dt0 = jnp.exp(jax.random.uniform(k[14], (NS, 2, SSM_HEADS), f32, math.log(1e-3), math.log(1e-1)))
    return {
        'x': nrm(0, (BATCH, SEQ, D), 1.0),
        'c': nrm(1, (BATCH, D), 1.0),
        'ctx': nrm(2, (BATCH, CTX_LEN, D), 1.0),
        'c_ctx': nrm(3, (D,), 1.0),
        'ada_w': nrm(4, (DEPTH, D, 6 * D), 0.5 * D ** -0.5),
        'ada_b': nrm(5, (DEPTH, 6 * D), 0.02),
        'norm_mix_pre': gain(6, (DEPTH, D)),
        'norm_mix_post': gain(7, (DEPTH, D)),
        'norm_ffn_pre': gain(8, (DEPTH, D)),
        'norm_ffn_post': gain(9, (DEPTH, D)),
        'ssm_w_in': nrm(10, (NS, D, D_IN_PROJ), D ** -0.5),
        'ssm_conv_w': nrm(11, (NS, SSM_CONV, CONV_DIM), SSM_CONV ** -0.5),
        'ssm_conv_b': nrm(12, (NS, CONV_DIM), 0.02),
        'ssm_dt_bias': dt0 + jnp.log(-jnp.expm1(-dt0)),
        'ssm_a_log': jnp.log(jax.random.uniform(k[15], (NS, 2, SSM_HEADS), f32, 1.0, 16.0)),
        'ssm_d': gain(16, (NS, SSM_HEADS)),
        'ssm_norm': gain(17, (NS, D_INNER)),
        'ssm_w_out': nrm(18, (NS, D_INNER, D), D_INNER ** -0.5),
        'cv_w_in': nrm(19, (NC, D, 2 * D), D ** -0.5),
        'cv_b_in': nrm(20, (NC, 2 * D), 0.02),
        'cv_dw_w': nrm(21, (NC, CONF_WIDTH, D), CONF_WIDTH ** -0.5),
        'cv_dw_b': nrm(22, (NC, D), 0.02),
        'cv_ln_g': gain(23, (NC, D)),
        'cv_ln_b': nrm(24, (NC, D), 0.02),
        'cv_w_out': nrm(25, (NC, D, D), D ** -0.5),
        'cv_b_out': nrm(26, (NC, D), 0.02),
        'router_w': nrm(27, (DEPTH, D, E), D ** -0.5),
        'router_b': nrm(28, (DEPTH, E), 0.01),
        'exp_w_gate': nrm(29, (DEPTH, E, D, D_EXPERT), D ** -0.5),
        'exp_w_up': nrm(30, (DEPTH, E, D, D_EXPERT), D ** -0.5),
        'exp_w_down': nrm(31, (DEPTH, E, D_EXPERT, D), D_EXPERT ** -0.5),
        'sh_w_gate': nrm(32, (DEPTH, D, D_SHARED), D ** -0.5),
        'sh_w_up': nrm(33, (DEPTH, D, D_SHARED), D ** -0.5),
        'sh_w_down': nrm(34, (DEPTH, D_SHARED, D), D_SHARED ** -0.5),
    }

def reference(x, c, ctx, c_ctx, ada_w, ada_b, norm_mix_pre, norm_mix_post, norm_ffn_pre, norm_ffn_post,
              ssm_w_in, ssm_conv_w, ssm_conv_b, ssm_dt_bias, ssm_a_log, ssm_d, ssm_norm, ssm_w_out,
              cv_w_in, cv_b_in, cv_dw_w, cv_dw_b, cv_ln_g, cv_ln_b, cv_w_out, cv_b_out,
              router_w, router_b, exp_w_gate, exp_w_up, exp_w_down, sh_w_gate, sh_w_up, sh_w_down):
    bsz, seq, d = x.shape
    rows = seq // GRID_W
    silu_c = jax.nn.silu(c)
    silu_cc = jax.nn.silu(c_ctx)
    xc = ctx
    for i in range(DEPTH):
        is_ssm = i % N_MIXERS == 0
        j = i // N_MIXERS
        ctx_later = any(m % N_MIXERS == 0 for m in range(i + 1, DEPTH))
        ctx_in = is_ssm or ctx_later
        sh1, sc1, g1, sh2, sc2, g2 = jnp.split((silu_c @ ada_w[i] + ada_b[i])[:, None, :], 6, axis=-1)
        hl = rms_norm(x, norm_mix_pre[i]) * (1 + sc1) + sh1
        if ctx_in:
            csh1, csc1, cg1, csh2, csc2, cg2 = jnp.split(silu_cc @ ada_w[i] + ada_b[i], 6)
            hc = rms_norm(xc, norm_mix_pre[i]) * (1 + csc1) + csh1
        if is_ssm:
            yl, yc = mamba_mixer(hl, hc, ssm_w_in[j], ssm_conv_w[j], ssm_conv_b[j], ssm_dt_bias[j],
                                 ssm_a_log[j], ssm_d[j], ssm_norm[j], ssm_w_out[j], ctx_later)
        else:
            cv = (cv_w_in[j], cv_b_in[j], cv_dw_w[j], cv_dw_b[j], cv_ln_g[j], cv_ln_b[j], cv_w_out[j], cv_b_out[j])
            yl = conformer_mixer(hl, rows, GRID_W, *cv)
            yc = conformer_mixer(hc, 1, hc.shape[1], *cv) if ctx_later else None
        x = x + g1 * rms_norm(yl, norm_mix_post[i])
        hl = rms_norm(x, norm_ffn_pre[i]) * (1 + sc2) + sh2
        moe_w = (router_w[i], router_b[i], exp_w_gate[i], exp_w_up[i], exp_w_down[i],
                 sh_w_gate[i], sh_w_up[i], sh_w_down[i])
        if ctx_later:
            xc = xc + cg1 * rms_norm(yc, norm_mix_post[i])
            hc = rms_norm(xc, norm_ffn_pre[i]) * (1 + csc2) + csh2
            f = moe_ffn(jnp.concatenate([hl.reshape(-1, d), hc.reshape(-1, d)], axis=0), *moe_w)
            fl = f[: bsz * seq].reshape(x.shape)
            fc = f[bsz * seq:].reshape(xc.shape)
            xc = xc + cg2 * rms_norm(fc, norm_ffn_post[i])
        else:
            fl = moe_ffn(hl.reshape(-1, d), *moe_w).reshape(x.shape)
        x = x + g2 * rms_norm(fl, norm_ffn_post[i])
    return x


_drawn_inputs = setup_inputs


def setup_inputs(seed=0):
    import zlib

    import numpy as np

    out = dict(_drawn_inputs(seed))
    spreads = {}
    factors = {'cv_b_in': 3.642, 'cv_dw_b': 2.727, 'cv_ln_b': 3.303, 'cv_b_out': 2.745}
    for name, (base, spread) in spreads.items():
        noise = np.random.default_rng([zlib.crc32(name.encode()), seed]).standard_normal(out[name].shape)
        drawn = base * np.exp(spread * noise) if base else spread * noise
        out[name] = jnp.asarray(drawn.astype(out[name].dtype))
    for name, factor in factors.items():
        out[name] = (out[name] * factor).astype(out[name].dtype)
    return out
```

```python
from contextlib import ExitStack

import numpy as np
import concourse.bass as bass
from concourse import mybir

F32 = mybir.dt.float32
F32R = mybir.dt.float32r
BF16 = mybir.dt.bfloat16
I32 = mybir.dt.int32
ALU = mybir.AluOpType
ACT = mybir.ActivationFunctionType
AX = mybir.AxisListType
ds = bass.ds

P = 128
D = 1024
KD = D // P
T = 256
TT = T // P
G = 8
R = 4
PH = 64
GW = R * PH
TAPS = 5
WG = 2 * P + P + P + GW
EPS = 1e-6
E = 64
F = 256
CAP = 64
NOV = 34
NB = E + NOV
NPAIR = NB // 2
TAP31 = 31
ROW = 64
NROW = T // ROW
PADROW = ROW + TAP31 - 1
ADA_G = 10 * D // G
ADA_C = ADA_G // P
BIG = 1e30
GU_PAIR = 8192
DN_PAIR = 4096

C_ID, C_TU, C_TL, C_ONE, C_MF, C_MB = (P * i for i in range(6))
C_I64 = 6 * P
C_IOV = C_I64 + 64
C_LT8 = C_IOV + NOV
C_PIX = C_LT8 + 64
C_IE = C_PIX + 1
C_N = C_IE + E

V_NPRE = 0
V_BSH = V_NPRE + KD
V_BSC = V_BSH + KD
V_ADAB = V_BSC + KD
V_ONE = V_ADAB + 80
V_MUL = V_ONE + 80
V_CONV = V_MUL + 80
V_SN = V_CONV + G * 4 * (TAPS + 1)
V_NPRE1 = V_SN + 2 * G
V_CBI = V_NPRE1 + KD
V_DW = V_CBI + 2 * KD
V_DWB = V_DW + KD * TAP31
V_LNG = V_DWB + KD
V_LNB = V_LNG + KD
V_N = V_LNB + KD

R_SD = 0
R_RB = 32
R_BO = R_RB + 2 * E
R_N = R_BO + D


class Chain:

    def __init__(self, eng, sem):
        self.eng, self.sem, self.base, self.n = eng, sem, 0, 0

    def at(self, base):
        self.base, self.n = base, 0

    def post(self, ins):
        ins.then_inc(self.sem, 1)
        self.n += 1

    def link(self, ins):
        self.post(ins)
        self.eng.wait_ge(self.sem, self.base + self.n)


def signal(eng, ins, sem, value):
    ins.then_inc(sem, 1)
    eng.wait_ge(sem, value)


class Core:

    def __init__(self, nc, ctx):
        self.nc, self.ctx, self.stage_sems = nc, ctx, []

    def sb(self, name, shape, dt=F32, ctx=None):
        return (ctx or self.ctx).enter_context(self.nc.sbuf_tensor(name, shape, dt))

    def ps(self, name, shape, dt=F32):
        return self.ctx.enter_context(self.nc.psum_tensor(name, shape, dt))

    def sem(self, name):
        self.stage_sems.append(self.nc.alloc_semaphore(name=name))
        return self.stage_sems[-1]

    def release(self):
        self.nc.clear_and_free_semaphores(self.stage_sems)
        self.nc.all_engine_barrier()
        self.stage_sems = []


def build(nc, a):
    with ExitStack() as ctx:
        c = Core(nc, ctx)
        c.gu = c.sb("gu", [P, 2 * GU_PAIR])
        c.dn = c.sb("dn", [P, 2 * DN_PAIR])
        c.x = c.sb("x", [P, TT, D])
        c.hT = c.sb("hT", [P, KD, 2 * T])
        c.cst = c.sb("cst", [P, C_N])
        c.vec = c.sb("vec", [P, V_N])
        c.rows = c.sb("rows", [P, R_N])
        c.adac = c.sb("adac", [P, 10 * (G + 1)])
        c.small = c.sb("small", [P, 64])
        c.pt = c.ps("pt", [P, 4, 512])
        c.pa = c.ps("pa", [P, 4, 512])
        c.const_landed = ctx.enter_context(nc.semaphore("const_landed"))
        with ExitStack() as s:
            b = ssm_buffers(c, s)
            modulate(nc, c, a, b)
            ssd(nc, c, a, b)
            c.release()
        for layer in range(2):
            with ExitStack() as s:
                m = moe_buffers(c, s, layer)
                if layer == 0:
                    ada_rows(nc, c, a, m)
                router(nc, c, a, m, layer)
                experts(nc, c, a, m, layer)
                ffn_end(nc, c, a, m, layer)
            if layer == 0:
                c.release()
                with ExitStack() as s:
                    conformer(nc, c, a, s)
                    c.release()



class Bag:
    pass


def ssm_buffers(c, s):
    b = Bag()
    sb = lambda name, shape, dt=F32: c.sb(name, shape, dt, s)
    b.cin = sb("conv_in", [P, 4, 2, T + TAPS - 1])
    b.cout = sb("conv_out", [P, 4, 2 * T])
    b.xs = sb("xs", [P, 4, GW])
    b.bt = sb("bt", [P, 4, P])
    b.cb = sb("cb", [P, 2, P])
    b.zs = sb("zs", [P, TT, GW])
    b.dec = sb("decay", [P, 2, R, 2, P])
    b.xu = sb("xu", [P, 6, GW])
    b.hs = sb("hs", [P, 4, GW])
    b.htmp = sb("htmp", [P, GW])
    b.y = sb("y", [P, TT, GW])
    b.ytmp = sb("ytmp", [P, TT, GW])
    b.yT = sb("yT", [P, 2, T])
    b.dt = sb("dtT", [P, 2, 4, 32])
    b.cs = sb("cs", [P, 2, 4, 32])
    b.ecs = sb("ecs", [P, 2, 4, 32])
    b.tot = sb("tot", [P, 2, 4, 32])
    b.uw = sb("uw", [P, 2, 4, 32])
    b.da = sb("daT", [P, 4, 64])
    b.csT = sb("csT", [64, T])
    b.col = sb("dtcol", [64, 4])
    b.adaacc = sb("adaacc", [P, ADA_G])
    b.cv = sb("cv", [P, KD, 2])
    b.scv = sb("scv", [P, KD, 2])
    b.mix = sb("mixcols", [P, 2, KD, 2])
    b.nrm = sb("nrm", [P, 8])
    return b


def modulate(nc, c, a, b):
    pt = c.pt
    w_landed = [c.sem(f"ada_landed{i}") for i in range(4)]
    cv_landed, x_landed, dtw_landed, scr_done = (c.sem(n) for n in ("cv_landed", "x_landed", "dtw_landed", "scr_done"))
    cv_ready, row_ps, row_sb, col_ps, mix_ready = (c.sem(n) for n in ("cv_ready", "row_ps", "row_sb", "col_ps", "mix_ready"))
    sumsq, rms_in, rms_sq, xn_ready, xt_ps, ht_act, ht_dve = (c.sem(n) for n in ("sumsq", "rms_in", "rms_sq", "xn_ready", "xt_ps", "ht_act", "ht_dve"))
    dt_ps, dt_z, dt_e, dt_u, dt_ln, dt_done, dtT_ps, dtT_sb, cs_ps, cs_sb, csT_sb, e_ready = (
        c.sem(n) for n in ("dt_ps", "dt_z", "dt_e", "dt_u", "dt_ln", "dt_done", "dtT_ps", "dtT_sb", "cs_ps", "cs_sb", "csT_sb", "e_ready"))
    mod_dve, mod_act = c.sem("mod_dve"), c.sem("mod_act")
    b.scr_done = scr_done
    b.win_landed = [c.sem(f"win_landed{i}") for i in range(2)]
    b.wout_landed = [c.sem(f"wout_landed{i}") for i in range(2)]
    b.csb_landed = c.sem("csb_landed")

    xn = c.dn[:, 0:4 * D].rearrange("p (q d) -> p q d", q=4)
    xc = b.dec[:].rearrange("p a r q l -> p (a r q l)")
    xq = [xc[:, 0:D], xc[:, D:2 * D], c.x[:, 0, :], c.x[:, 1, :]]
    wdt = c.dn[:, 4 * D:4 * D + KD * 64].rearrange("p (k n) -> p k n", k=KD)
    rows = b.cout[0:2].rearrange("p a b -> p (a b)")
    tmp = [c.gu[0:64, 6144 + 512 * i:6144 + 512 * (i + 1)] for i in range(4)]
    more = [c.gu[0:64, 14336 + 512 * i:14336 + 512 * (i + 1)] for i in range(3)]
    z, m, e, u = tmp
    d, ln, dtD = more
    ident = c.cst[:, C_ID:C_ID + P]

    with nc.Block() as block:
        @block.sync
        def _(sp):
            sp.dma_start(b.cv[:], a["cvec"]).then_inc(cv_landed, 16)
            sp.dma_start(c.gu[:, 0:4096], a["ada_first"][0]).then_inc(w_landed[0], 16)
            for t in range(2):
                sp.dma_start(xq[t], a["ctx"][t]).then_inc(x_landed, 16)
                sp.dma_start(xq[2 + t], a["x"][t]).then_inc(x_landed, 16)
            sp.dma_start(c.cst[:], a["consts"]).then_inc(c.const_landed, 16)
            sp.dma_start(c.vec[:], a["vecs"]).then_inc(c.const_landed, 16)
            sp.dma_start(c.rows[:], a["rows"].partition_broadcast(P)).then_inc(c.const_landed, 16)
            sp.dma_start(b.col[:, 0:2], a["dtcols"]).then_inc(c.const_landed, 16)
            for n in range(1, 4):
                sp.dma_start(c.gu[:, 4096 * n:4096 * (n + 1)], a["ada_first"][n]).then_inc(w_landed[n], 16)
            sp.dma_start(wdt, a["w_dt"]).then_inc(dtw_landed, 16)
            sp.wait_ge(row_ps, 2)
            sp.dma_start(c.gu[:, 0:KD * WG], a["w_in"][0]).then_inc(b.win_landed[0], 16)
            sp.wait_ge(row_ps, 4)
            sp.dma_start(c.gu[:, GU_PAIR:GU_PAIR + KD * WG], a["w_in"][1]).then_inc(b.win_landed[1], 16)
            sp.wait_ge(xt_ps, 8)
            sp.dma_start(c.dn[:, 0:2 * D], a["w_out"][0]).then_inc(b.wout_landed[0], 16)
            sp.wait_ge(csT_sb, 1)
            sp.dma_start(a["cs_scr"], b.csT[:]).then_inc(scr_done, 16)
            sp.wait_ge(scr_done, 16)
            for dr in range(2):
                sp.dma_start(b.dec[:, dr].rearrange("p r q l -> p (r q l)"),
                             a["cs_scr"][32 * dr:32 * dr + R].rearrange("r l -> (r l)").partition_broadcast(P)).then_inc(b.csb_landed, 16)

        @block.tensor
        def _(pe):
            pe.wait_ge(cv_ready, 1)
            for n in range(4):
                pe.wait_ge(w_landed[n], 16)
                w = c.gu[:, 4096 * n:4096 * (n + 1)].rearrange("p (k n) -> p k n", k=KD)
                for k in range(KD):
                    mm = pe.matmul(pt[0:2, n, :], b.scv[:, k, :], w[:, k, :], start=k == 0, stop=k == KD - 1)
                mm.then_inc(row_ps, 1)
            pe.wait_ge(c.const_landed, 64)
            pe.wait_ge(row_sb, 4)
            for j in range(16):
                mm = pe.transpose(pt[:, 0, 2 * j:2 * j + 2], rows[:, P * j:P * (j + 1)], ident[0:2, 0:2])
            mm.then_inc(col_ps, 1)
            for q in range(4):
                pe.wait_ge(xn_ready, q + 1)
                for h in range(2):
                    if q == 0:
                        pe.wait_ge(mix_ready, 1)
                    if q >= 1:
                        pe.wait_ge(ht_act, 2 * (q - 1) + h + 1)
                        pe.wait_ge(ht_dve, 2 * (q - 1) + h + 1)
                    for k in range(4 * h, 4 * h + 4):
                        mm = pe.transpose(pt[:, 2 * h + k % 2, P * (k // 2 % 2):P * (k // 2 % 2 + 1)], xn[:, q, P * k:P * (k + 1)], ident)
                    mm.then_inc(xt_ps, 1)
            pe.wait_ge(dtw_landed, 16)
            pe.wait_ge(ht_act, 8)
            pe.wait_ge(ht_dve, 8)
            for k in range(KD):
                mm = pe.matmul(pt[0:64, 0, :], wdt[:, k, :], c.hT[:, k, :], start=k == 0, stop=k == KD - 1)
            mm.then_inc(dt_ps, 1)
            pe.wait_ge(dt_done, 2)
            for i, src in enumerate((dtD, z)):
                for q in range(4):
                    mm = pe.transpose(pt[:, 1, 256 * i + 64 * q:256 * i + 64 * (q + 1)], src[:, P * q:P * (q + 1)], ident[0:64, 0:64])
            mm.then_inc(dtT_ps, 1)
            pe.wait_ge(dtT_sb, 1)
            tri = [c.cst[:, C_TU:C_TU + P], c.cst[:, C_TL:C_TL + P]]
            for dr in range(2):
                pe.matmul(pt[:, 2, P * dr:P * (dr + 1)], tri[dr], b.da[:, :, 32 * dr:32 * (dr + 1)], start=True, stop=True)
            pe.matmul(pt[:, 2, 256:512], c.cst[:, C_ONE:C_ONE + P], b.da[:].rearrange("p q n -> p (q n)"), start=True, stop=True).then_inc(cs_ps, 1)
            for dr in range(2):
                for q in range(2):
                    mm = pe.matmul(pt[32 * dr:32 * (dr + 1), 3, P * q:P * (q + 1)], b.da[:, 2 + q, 32 * dr:32 * (dr + 1)], tri[dr], start=True, stop=True)
            mm.then_inc(cs_ps, 1)
            for n in range(4):
                mm = pe.matmul(c.pa[:, n, :], b.cin[:, 0, 0, 0:P], c.hT[:, 0, :], start=True, stop=False, skip_group_check=True)
            mm.then_inc(cs_ps, 1)

        @block.scalar
        def _(act):
            ch = Chain(act, mod_act)
            act.wait_ge(cv_landed, 16)
            signal(act, act.activation(b.scv[:].rearrange("p k n -> p (k n)"), b.cv[:].rearrange("p k n -> p (k n)"), ACT.Silu), cv_ready, 1)
            act.wait_ge(x_landed, 64)
            for q in range(4):
                signal(act, act.activation(b.cin[:].rearrange("p a b c -> p (a b c)")[:, 0:D], xq[q], ACT.Square, accum_out=b.nrm[:, q:q + 1]), sumsq, q + 1)
            for n in range(4):
                act.wait_ge(row_ps, n + 1)
                signal(act, act.copy(rows[:, 512 * n:512 * (n + 1)], pt[0:2, n, :]), row_sb, n + 1)
            act.wait_ge(rms_in, 1)
            signal(act, act.activation(b.nrm[:, 4:8], b.nrm[:, 0:4], ACT.Sqrt), rms_sq, 1)
            act.wait_ge(mix_ready, 1)
            for q in range(4):
                s = 1 if q < 2 else 0
                for h in range(2):
                    act.wait_ge(xt_ps, 2 * q + h + 1)
                    for k in (4 * h, 4 * h + 2):
                        ins = act.activation(c.hT[:, k, P * q:P * (q + 1)], pt[:, 2 * h, P * (k // 2 % 2):P * (k // 2 % 2 + 1)], ACT.Identity,
                                             bias=b.mix[:, 0, k, s:s + 1], scale=b.mix[:, 1, k, s:s + 1])
                        if k == 4 * h:
                            ch.post(ins)
                    signal(act, ins, ht_act, 2 * q + h + 1)
            act.wait_ge(c.const_landed, 64)
            ch.link(act.activation(b.col[:, 2:3], b.col[:, 1:2], ACT.Exp))
            act.wait_ge(dt_z, 1)
            ch.link(act.activation(e, z, ACT.Abs))
            signal(act, act.activation(e, e, ACT.Exp, scale=-1.0), dt_e, 1)
            act.wait_ge(dt_u, 1)
            signal(act, act.activation(ln, u, ACT.Ln), dt_ln, 1)
            act.wait_ge(cs_sb, 1)
            cols = lambda t: t[:].rearrange("p a q n -> p (a q n)")
            ch.post(act.activation(cols(b.ecs), cols(b.cs), ACT.Exp))
            ch.post(act.activation(cols(b.uw), cols(b.uw), ACT.Exp))
            signal(act, act.activation(cols(b.tot), cols(b.tot), ACT.Exp), e_ready, 1)

        @block.vector
        def _(dve):
            ch = Chain(dve, mod_dve)
            dve.wait_ge(sumsq, 4)
            ch.post(dve.memset(b.adaacc[:], 0.0))
            ch.link(dve.memset(b.cin[:], 0.0))
            signal(dve, dve.tensor_scalar(b.nrm[:, 0:4], b.nrm[:, 0:4], 1.0 / D, EPS, ALU.mult, ALU.add), rms_in, 1)
            dve.wait_ge(rms_sq, 1)
            ch.link(dve.reciprocal(b.nrm[:, 4:8], b.nrm[:, 4:8]))
            for q in range(4):
                signal(dve, dve.tensor_scalar(xn[:, q, :], xq[q], b.nrm[:, 4 + q:5 + q], None, ALU.mult), xn_ready, q + 1)
            dve.wait_ge(c.const_landed, 64)
            dve.wait_ge(col_ps, 1)
            v = lambda o, n: c.vec[:, o:o + n].unsqueeze(2).broadcast_to([P, n, 2])
            cols = pt[:, 0, 0:32].rearrange("p (j n) -> p j n", n=2)
            ch.post(dve.tensor_tensor(b.mix[:, 0], cols[:, 0:KD], v(V_BSH, KD), ALU.add))
            ch.link(dve.tensor_tensor(b.mix[:, 1], cols[:, KD:2 * KD], v(V_BSC, KD), ALU.add))
            signal(dve, dve.scalar_tensor_tensor(out=b.mix[:, 1], in0=b.mix[:, 1], scalar=1.0, in1=v(V_NPRE, KD), op0=ALU.add, op1=ALU.mult), mix_ready, 1)
            for q in range(4):
                s = 1 if q < 2 else 0
                for h in range(2):
                    dve.wait_ge(xt_ps, 2 * q + h + 1)
                    for k in (4 * h + 1, 4 * h + 3):
                        ins = dve.tensor_scalar(c.hT[:, k, P * q:P * (q + 1)], pt[:, 2 * h + 1, P * (k // 2 % 2):P * (k // 2 % 2 + 1)],
                                                b.mix[:, 1, k, s:s + 1], b.mix[:, 0, k, s:s + 1], ALU.mult, ALU.add)
                        if k == 4 * h + 1:
                            ch.post(ins)
                    signal(dve, ins, ht_dve, 2 * q + h + 1)
            dve.wait_ge(dt_ps, 1)
            dve.wait_ge(row_ps, 4)
            signal(dve, dve.tensor_scalar(z, pt[0:64, 0, :], b.col[:, 0:1], None, ALU.add), dt_z, 1)
            ch.link(dve.tensor_scalar(m, z, 0.0, None, ALU.max))
            dve.wait_ge(dt_e, 1)
            signal(dve, dve.tensor_scalar(u, e, 1.0, None, ALU.add), dt_u, 1)
            ch.link(dve.tensor_scalar(d, u, 1.0, None, ALU.subtract))
            ch.link(dve.tensor_tensor(d, e, d, ALU.subtract))
            dve.wait_ge(dt_ln, 1)
            ch.link(dve.reciprocal(u, u))
            ch.link(dve.tensor_tensor(d, d, u, ALU.mult))
            ch.link(dve.tensor_tensor(m, m, ln, ALU.add))
            signal(dve, dve.tensor_tensor(dtD, m, d, ALU.add), dt_done, 1)
            signal(dve, dve.tensor_scalar(z, dtD, b.col[:, 2:3], -1.0, ALU.mult, ALU.mult), dt_done, 2)
            dve.wait_ge(dtT_ps, 1)
            for dr in range(2):
                ch.post(dve.tensor_copy(b.dt[:, dr], pt[:, 1, 0:256].rearrange("p (q a n) -> p a q n", q=4, a=2)[:, dr]))
            ins = dve.tensor_copy(b.da[:].rearrange("p q n -> p (q n)"), pt[:, 1, 256:512])
            signal(dve, ins, dtT_sb, 1)
            dve.wait_ge(cs_ps, 1)
            for dr in range(2):
                ch.post(dve.tensor_copy(b.cs[:, dr].rearrange("p q n -> p (q n)"), pt[:, 2, P * dr:P * (dr + 1)]))
            for dr in range(2):
                ch.link(dve.tensor_copy(b.tot[:, dr], pt[:, 2, 256:512].rearrange("p (q a n) -> p a q n", q=4, a=2)[:, dr]))
            signal(dve, dve.tensor_tensor(b.uw[:].rearrange("p a q n -> p (a q n)"), b.tot[:].rearrange("p a q n -> p (a q n)"),
                                          b.cs[:].rearrange("p a q n -> p (a q n)"), ALU.subtract), cs_sb, 1)
            dve.wait_ge(cs_ps, 2)
            signal(dve, dve.tensor_copy(b.csT[:], pt[0:64, 3, 0:256]), csT_sb, 1)
            dve.wait_ge(e_ready, 1)
            ch.link(dve.tensor_tensor(b.uw[:].rearrange("p a q n -> p (a q n)"), b.uw[:].rearrange("p a q n -> p (a q n)"),
                                      b.dt[:].rearrange("p a q n -> p (a q n)"), ALU.mult))



def ssd(nc, c, a, b):
    pt, pa = c.pt, c.pa
    XC, BC, CC = 0, 2, 3
    proj_ps = c.sem("proj_ps")
    conv_in = c.sem("conv_in_ready")
    conv_sum = c.sem("conv_sum")
    conv_act = c.sem("conv_act")
    z_ready, ada_col, ada_used = (c.sem(n) for n in ("z_ready", "ada_col", "ada_used"))
    tr_ps, tr_sb = c.sem("tr_ps"), c.sem("tr_sb")
    xu_ready, st_ps, st_ready = c.sem("xu_ready"), c.sem("st_ps"), c.sem("st_ready")
    diff_ready, exp_ready, m_ready = c.sem("diff_ready"), c.sem("exp_ready"), c.sem("m_ready")
    y_ps, y_sum, y_gated, ysq, yms, yrt, yn_ready = (c.sem(n) for n in ("y_ps", "y_sum", "y_gated", "ysq", "yms", "yrt", "yn_ready"))
    yT_ps, yT_sb, out_ps = c.sem("yT_ps"), c.sem("yT_sb"), c.sem("out_ps")
    ada_landed = [c.sem(f"ada_tile{i}") for i in range(4)]
    ssd_dve, ssd_act = c.sem("ssd_dve"), c.sem("ssd_act")
    ident = c.cst[:, C_ID:C_ID + P]
    ada_tile = [c.dn[:, 4096:4096 + ADA_G], c.dn[:, 4096 + ADA_G:4096 + 2 * ADA_G],
                c.gu[:, 6144:6144 + ADA_G], c.gu[:, 14336:14336 + ADA_G]]
    win = [c.gu[:, GU_PAIR * s:GU_PAIR * s + KD * WG].rearrange("p (k n) -> p k n", k=KD) for s in range(2)]
    wout = [c.dn[:, 2 * D * s:2 * D * (s + 1)].rearrange("p (j n) -> p j n", j=2) for s in range(2)]
    heads = lambda t, dr, q0, q1, g: t[:, dr, q0:q1, ds(R * g, R)]
    wide = lambda ap, q: ap.unsqueeze(3).broadcast_to([P, q, R, PH])
    as_heads = lambda ap: ap.rearrange("p q (r n) -> p q r n", r=R)

    def over_groups(eng, body):
        with eng.Fori(0, G // 2 - 1) as i:
            body(2 * i, 0, True, True)
            body(2 * i + 1, 1, True, True)
        body(G - 2, 0, True, False)
        body(G - 1, 1, False, False)

    with nc.Block() as block:
        @block.sync
        def _(sp):
            def group(g, slot, following, two_following):
                if two_following:
                    sp.wait_ge(proj_ps, 5 * g + 5)
                    sp.dma_start(c.gu[:, GU_PAIR * slot:GU_PAIR * slot + KD * WG],
                                 a["w_in"][ds(g + 2, 1)].rearrange("g p n -> (g p) n")).then_inc(b.win_landed[slot], 16)
                if following:
                    sp.wait_ge(y_ps, g + 1)
                    sp.dma_start(c.dn[:, 2 * D * (1 - slot):2 * D * (2 - slot)],
                                 a["w_out"][ds(g + 1, 1)].rearrange("g p n -> (g p) n")).then_inc(b.wout_landed[1 - slot], 16)
                    for dr in range(2):
                        sp.dma_start(b.dec[:, dr].rearrange("p r q l -> p (r q l)"),
                                     a["cs_scr"][ds(32 * dr + R * (g + 1), R)].rearrange("r l -> (r l)").partition_broadcast(P)).then_inc(b.csb_landed, 16)
            over_groups(sp, group)

        @block.gpsimd
        def _(pool):
            def group(g, slot, following, two_following):
                for k in range(KD):
                    if k >= 4:
                        pool.wait_ge(ada_used, KD * g + k - 3)
                    elif not isinstance(g, int) or g > 0:
                        pool.wait_ge(ada_used, KD * g + k - 3)
                    pool.dma_start(ada_tile[k % 4], a["ada_rest"][ds(KD * g + k, 1)].rearrange("g p n -> (g p) n")).then_inc(ada_landed[k % 4], 16)
            group(0, 0, True, True)
            with pool.Fori(1, G) as g:
                group(g, 0, True, True)

        @block.tensor
        def _(pe):
            def proj(g, slot, part):
                w = win[slot]
                if part == 0:
                    pe.wait_ge(b.win_landed[slot], 16 * (g // 2) + 16 if isinstance(g, int) else 8 * (g - slot) + 16)
                if part < 3:
                    for k in range(KD):
                        mm = pe.matmul(pt[:, 0, :], w[:, k, P * part:P * (part + 1)], c.hT[:, k, :], start=k == 0, stop=k == KD - 1)
                elif part == 3:
                    for k in range(KD):
                        mm = pe.matmul(pt[:, 1, 0:T], w[:, k, 3 * P:4 * P], c.hT[:, k, T:2 * T], start=k == 0, stop=k == KD - 1)
                else:
                    for t in range(TT):
                        for k in range(KD):
                            mm = pe.matmul(pt[:, 3, GW * t:GW * (t + 1)], c.hT[:, k, T + P * t:T + P * (t + 1)], w[:, k, 4 * P:4 * P + GW],
                                           start=k == 0, stop=k == KD - 1)
                mm.then_inc(proj_ps, 1)

            def ada(g):
                for j in range(ADA_C):
                    mm = pe.matmul(pt[:, 3, T + j:T + j + 1], b.adaacc[:, P * j:P * (j + 1)], c.cst[:, C_ONE:C_ONE + 1], start=True, stop=True)
                mm.then_inc(ada_col, 1)

            def group(g, slot, following, two_following):
                pe.wait_ge(conv_act, 4 * g + 4)
                for ch2 in range(2):
                    for q in range(4):
                        mm = pe.transpose(pt[:, q // 2, GW * (q % 2) + P * ch2:GW * (q % 2) + P * (ch2 + 1)], b.cout[:, XC + ch2, P * q:P * (q + 1)], ident)
                mm.then_inc(tr_ps, 1)
                for q in range(4):
                    mm = pe.transpose(pt[:, 2, P * q:P * (q + 1)], b.cout[:, BC, P * q:P * (q + 1)], ident)
                mm.then_inc(tr_ps, 1)
                pe.wait_ge(z_ready, g + 1)
                ada(g)
                for q in range(2):
                    mm = pe.matmul(pt[:, 3, P * q:P * (q + 1)], b.cout[:, BC, T + P * q:T + P * (q + 1)], b.cout[:, CC, T + P * q:T + P * (q + 1)], start=True, stop=True)
                mm.then_inc(tr_ps, 1)
                if following:
                    pe.wait_ge(tr_sb, 4 * g + 1)
                    proj(g + 1, 1 - slot, 0)
                pe.wait_ge(tr_sb, 4 * g + 4)
                pe.wait_ge(xu_ready, g + 1)
                for n, q in enumerate((0, 1, 2, 1, 0, 3)):
                    u = (0, 1, 2, 4, 3, 5)[n]
                    mm = pe.matmul(pt[:, 1 + n // 2, GW * (n % 2):GW * (n % 2 + 1)], b.bt[:, q, :], b.xu[:, u, :], start=True, stop=True)
                mm.then_inc(st_ps, 1)
                if following:
                    pe.wait_ge(conv_in, 4 * g + 5)
                    proj(g + 1, 1 - slot, 1)
                pe.wait_ge(st_ready, g + 1)
                for h in range(R):
                    pe.wait_ge(m_ready, g + 1)
                    for q in range(2):
                        pe.matmul(pt[:, 1, GW * q + PH * h:GW * q + PH * (h + 1)], b.dec[:, 0, h, q, :], b.xs[:, 2 + q, PH * h:PH * (h + 1)], start=True, stop=True)
                for dr in range(2):
                    for q in range(2):
                        mm = pe.matmul(pt[:, 2 + dr, GW * q:GW * (q + 1)], b.cout[:, CC, T + P * q:T + P * (q + 1)],
                                       b.hs[:, 2 * dr + (q if dr == 0 else 1 - q), :], start=True, stop=True)
                mm.then_inc(y_ps, 1)
                if following:
                    pe.wait_ge(conv_in, 4 * g + 6)
                    proj(g + 1, 1 - slot, 2)
                    pe.wait_ge(y_sum, g + 1)
                    proj(g + 1, 1 - slot, 3)
                pe.wait_ge(yn_ready, g + 1)
                for t in range(TT):
                    for j in range(2):
                        mm = pe.transpose(pt[:, 2, T * j + P * t:T * j + P * (t + 1)], b.y[:, t, P * j:P * (j + 1)], ident)
                mm.then_inc(yT_ps, 1)
                if following:
                    proj(g + 1, 1 - slot, 4)
                pe.wait_ge(yT_sb, g + 1)
                pe.wait_ge(b.wout_landed[slot], 16 * (g // 2) + 16 if isinstance(g, int) else 8 * (g - slot) + 16)
                for t in range(TT):
                    for h in range(2):
                        for j in range(2):
                            mm = pe.matmul(pa[:, 2 * t + h, :], b.yT[:, j, P * t:P * (t + 1)], wout[slot][:, j, 512 * h:512 * (h + 1)],
                                           start=False, stop=False, skip_group_check=True)
                mm.then_inc(out_ps, 1)

            for part in range(5):
                if part in (1, 2):
                    pe.wait_ge(conv_in, part)
                proj(0, 0, part)
            over_groups(pe, group)
            pe.wait_ge(ada_used, KD * G)
            ada(G)

        @block.scalar
        def _(act):
            ch = Chain(act, ssd_act)

            def take(g, part):
                act.wait_ge(proj_ps, 5 * g + part + 1)
                if not isinstance(g, int) or g > 0:
                    act.wait_ge(conv_sum, 4 * g + part - 3)
                if part < 3:
                    ins = act.copy(b.cin[:, part, :, 2:2 + T], pt[:, 0, :].rearrange("p (s l) -> p s l", s=2))
                else:
                    ins = act.copy(b.cin[:, part, 1, 2:2 + T], pt[:, 1, 0:T])
                signal(act, ins, conv_in, 4 * g + part + 1)

            def silu(g, part):
                act.wait_ge(conv_sum, 4 * g + part + 1)
                ap = b.cout[:, part, :] if part < 3 else b.cout[:, part, T:2 * T]
                signal(act, act.activation(ap, ap, ACT.Silu), conv_act, 4 * g + part + 1)

            def take_z(g):
                act.wait_ge(proj_ps, 5 * g + 5)
                if not isinstance(g, int) or g > 0:
                    act.wait_ge(y_gated, g)
                signal(act, act.activation(b.zs[:].rearrange("p t n -> p (t n)"), pt[:, 3, :], ACT.Silu), z_ready, g + 1)

            def group(g, slot, following, two_following):
                ch.at(3 * g)
                act.wait_ge(tr_ps, 3 * g + 1)
                for n in range(2):
                    signal(act, act.copy(b.xs[:, 2 * n:2 * n + 2, :].rearrange("p q n -> p (q n)"), pt[:, n, :]), tr_sb, 4 * g + n + 1)
                act.wait_ge(tr_ps, 3 * g + 2)
                signal(act, act.copy(b.bt[:].rearrange("p q n -> p (q n)"), pt[:, 2, :]), tr_sb, 4 * g + 3)
                act.wait_ge(tr_ps, 3 * g + 3)
                ch.link(act.copy(c.adac[:, ds(ADA_C * g, ADA_C)], pt[:, 3, T:T + ADA_C]))
                signal(act, act.copy(b.cb[:].rearrange("p q n -> p (q n)"), pt[:, 3, 0:2 * P]), tr_sb, 4 * g + 4)
                act.wait_ge(diff_ready, g + 1)
                e = b.dec[:].rearrange("p d r q l -> p (d r q l)")
                signal(act, act.activation(e, e, ACT.Exp), exp_ready, g + 1)
                if following:
                    take(g + 1, 0)
                    silu(g + 1, 0)
                    take(g + 1, 1)
                    silu(g + 1, 1)
                    take(g + 1, 2)
                act.wait_ge(y_gated, g + 1)
                for t in range(TT):
                    ins = act.activation(b.ytmp[:, t, :], b.y[:, t, :], ACT.Square, accum_out=b.nrm[:, t:t + 1])
                    if t == 0:
                        ch.link(ins)
                signal(act, ins, ysq, g + 1)
                act.wait_ge(yms, g + 1)
                signal(act, act.activation(b.nrm[:, 2:4], b.nrm[:, 0:2], ACT.Sqrt), yrt, g + 1)
                if following:
                    take(g + 1, 3)
                act.wait_ge(yT_ps, g + 1)
                for j in range(2):
                    ins = act.activation(b.yT[:, j, :], pt[:, 2, T * j:T * (j + 1)], ACT.Copy, scale=c.vec[:, ds(V_SN + 2 * g + j, 1)])
                    if j == 0:
                        ch.link(ins)
                signal(act, ins, yT_sb, g + 1)
                if following:
                    take_z(g + 1)
                    silu(g + 1, 2)
                    silu(g + 1, 3)
                assert ch.n == 3

            for part in range(4):
                take(0, part)
                silu(0, part)
            take_z(0)
            over_groups(act, group)
            act.wait_ge(ada_col, G + 1)
            ch.at(3 * G)
            ch.link(act.copy(c.adac[:, ADA_C * G:ADA_C * (G + 1)], pt[:, 3, T:T + ADA_C]))

        @block.vector
        def _(dve):
            ch = Chain(dve, ssd_dve)

            def taps(g, part):
                dve.wait_ge(conv_in, 4 * g + part + 1)
                if not isinstance(g, int) or g > 0:
                    dve.wait_ge(tr_ps if part < 3 else y_ps, 3 * g if part < 3 else g)
                s0 = 0 if part < 3 else 1
                w = lambda tap: c.vec[:, ds(V_CONV + (4 * g + part) * (TAPS + 1) + tap, 1)]
                out = b.cout[:, part, :].rearrange("p (s l) -> p s l", s=2)[:, s0:2, :]
                at = lambda tap: b.cin[:, part, s0:2, tap:tap + T]
                ch.link(dve.tensor_scalar(out, at(0), w(0), w(TAPS), ALU.mult, ALU.add))
                for tap in range(1, TAPS):
                    ins = dve.scalar_tensor_tensor(out=out, in0=at(tap), scalar=w(tap), in1=out, op0=ALU.mult, op1=ALU.add)
                    if tap < TAPS - 1:
                        ch.link(ins)
                    else:
                        signal(dve, ins, conv_sum, 4 * g + part + 1)

            def ada(g, k):
                dve.wait_ge(ada_landed[k % 4], 32 * g + 16 * (k // 4) + 16)
                if k == 0:
                    dve.wait_ge(ada_col, g + 1)
                if k == 0:
                    ins = dve.tensor_scalar(b.adaacc[:], ada_tile[0], b.scv[:, 0, 0:1], None, ALU.mult)
                else:
                    ins = dve.scalar_tensor_tensor(out=b.adaacc[:], in0=ada_tile[k % 4], scalar=b.scv[:, k, 0:1], in1=b.adaacc[:], op0=ALU.mult, op1=ALU.add)
                signal(dve, ins, ada_used, KD * g + k + 1)

            def group(g, slot, following, two_following):
                steps = 38 if following else 22
                ch.at(16 + 38 * g)
                dve.wait_ge(tr_sb, 4 * g + 2)
                for u0, q0, q1, dr in ((0, 0, 3, 0), (3, 0, 2, 1)):
                    ch.post(dve.tensor_tensor(as_heads(b.xu[:, u0:u0 + q1 - q0, :]), as_heads(b.xs[:, q0:q1, :]), wide(heads(b.uw, dr, q0, q1, g), q1 - q0), ALU.mult))
                signal(dve, dve.tensor_tensor(as_heads(b.xu[:, 5:6, :]), as_heads(b.xs[:, 3:4, :]), wide(heads(b.uw, 1, 3, 4, g), 1), ALU.mult), xu_ready, g + 1)
                dve.wait_ge(b.csb_landed, 32 * g + 32)
                for dr in range(2):
                    e = b.dec[:, dr]
                    csq = b.cs[:, dr, 2:4, ds(R * g, R)].rearrange("p q r -> p r q").unsqueeze(3).broadcast_to([P, R, 2, P])
                    ch.link(dve.tensor_tensor(e, e, csq, ALU.subtract))
                    mask = c.cst[:, (C_MF, C_MB)[dr]:(C_MF, C_MB)[dr] + P].unsqueeze(1).broadcast_to([P, 2 * R, P])
                    e2 = e.rearrange("p r q l -> p (r q) l")
                    ins = dve.tensor_tensor(e2, e2, mask, ALU.min)
                    if dr == 0:
                        ch.link(ins)
                signal(dve, ins, diff_ready, g + 1)
                ada(g, 0)
                ada(g, 1)
                if following:
                    taps(g + 1, 0)
                dve.wait_ge(st_ps, g + 1)
                S = lambda n: pt[:, 1 + n // 2, GW * (n % 2):GW * (n % 2 + 1)]
                head = lambda ap: ap.rearrange("p (r n) -> p r n", r=R)
                for dr in range(2):
                    dq = ((1, 2), (0, 3))[dr]
                    dec = lambda q: b.tot[:, dr, q, ds(R * g, R)].unsqueeze(2).broadcast_to([P, R, PH])
                    h1, h2 = b.hs[:, 2 * dr, :], b.hs[:, 2 * dr + 1, :]
                    ch.link(dve.tensor_tensor(head(b.htmp[:]), head(S(3 * dr)), dec(dq[0]), ALU.mult))
                    ch.link(dve.tensor_tensor(h1, b.htmp[:], S(3 * dr + 1), ALU.add))
                    ch.link(dve.tensor_tensor(head(b.htmp[:]), head(h1), dec(dq[1]), ALU.mult))
                    ins = dve.tensor_tensor(h2, b.htmp[:], S(3 * dr + 2), ALU.add)
                    if dr == 0:
                        ch.link(ins)
                signal(dve, ins, st_ready, g + 1)
                dve.wait_ge(exp_ready, g + 1)
                for dr in range(2):
                    dtq = b.dt[:, dr, 2:4, ds(R * g, R)].rearrange("p q r -> p r q").unsqueeze(3).broadcast_to([P, R, 2, P])
                    ch.link(dve.tensor_tensor(b.dec[:, dr], b.dec[:, dr], dtq, ALU.mult))
                ch.link(dve.tensor_tensor(b.dec[:, 0], b.dec[:, 0], b.dec[:, 1], ALU.add))
                dve.wait_ge(tr_sb, 4 * g + 4)
                m = b.dec[:, 0].rearrange("p r q l -> p r (q l)")
                signal(dve, dve.tensor_tensor(m, m, b.cb[:].rearrange("p q l -> p (q l)").unsqueeze(1).broadcast_to([P, R, 2 * P]), ALU.mult), m_ready, g + 1)
                ada(g, 2)
                ada(g, 3)
                if following:
                    taps(g + 1, 1)
                ada(g, 4)
                ada(g, 5)
                dve.wait_ge(y_ps, g + 1)
                y, yt = b.y[:], b.ytmp[:]
                bank = lambda n: pt[:, n, :].rearrange("p (q n) -> p q n", q=2)
                ch.post(dve.tensor_tensor(as_heads(y), as_heads(bank(2)), wide(heads(b.ecs, 0, 2, 4, g), 2), ALU.mult))
                ch.link(dve.tensor_tensor(as_heads(yt), as_heads(bank(3)), wide(heads(b.ecs, 1, 2, 4, g), 2), ALU.mult))
                ch.link(dve.tensor_tensor(y, y, yt, ALU.add))
                ch.link(dve.tensor_tensor(y, y, bank(1), ALU.add))
                skip = c.rows[:, ds(R_SD + R * g, R)].unsqueeze(1).unsqueeze(3).broadcast_to([P, 2, R, PH])
                signal(dve, dve.tensor_tensor(as_heads(yt), as_heads(b.xs[:, 2:4, :]), skip, ALU.mult), y_sum, g + 1)
                ch.link(dve.tensor_tensor(y, y, yt, ALU.add))
                dve.wait_ge(z_ready, g + 1)
                signal(dve, dve.tensor_tensor(y, y, b.zs[:], ALU.mult), y_gated, g + 1)
                dve.wait_ge(ysq, g + 1)
                signal(dve, dve.tensor_scalar(b.nrm[:, 0:2], b.nrm[:, 0:2], 1.0 / GW, EPS, ALU.mult, ALU.add), yms, g + 1)
                dve.wait_ge(yrt, g + 1)
                ch.link(dve.reciprocal(b.nrm[:, 4:6], b.nrm[:, 2:4]))
                for t in range(TT):
                    ins = dve.tensor_scalar(b.y[:, t, :], b.y[:, t, :], b.nrm[:, 4 + t:5 + t], None, ALU.mult)
                    if t == 0:
                        ch.link(ins)
                signal(dve, ins, yn_ready, g + 1)
                ada(g, 6)
                ada(g, 7)
                if following:
                    taps(g + 1, 2)
                    taps(g + 1, 3)
                assert ch.n == steps, ch.n

            for part in range(4):
                taps(0, part)
            over_groups(dve, group)



def moe_buffers(c, s, layer):
    m = Bag()
    sb = lambda name, shape, dt=F32: c.sb(f"{name}{layer}", shape, dt, s)
    m.bc = sb("bc", [P, 3, D])
    m.hr = sb("hr", [P, 2, TT, D], F32R)
    m.work = sb("work", [P, 2048])
    m.ys = sb("ys", [P, 2, D], F32R)
    m.sr = sb("sr", [P, TT, P], F32R)
    m.sb = sb("sb", [P, TT, P], BF16)
    m.st = sb("st", [P, T], F32R)
    m.rk = sb("rk", [P, NPAIR, TT, 2])
    m.wb = sb("wb", [P, NPAIR, TT, 3, 2], BF16)
    m.act = sb("act", [P, F])
    m.sg = sb("sg", [P, 2 * F])
    m.actT = sb("actT", [P, 2, T])
    m.wsl = sb("wsl", [P, 1])
    m.nrm = sb("mnrm", [P, 16])
    m.rw = sb("rw", [P, KD, E])
    m.idb = sb("idb", [P, P], BF16)
    m.tub = sb("tub", [P, P], BF16)
    m.oneb = sb("oneb", [P, P], BF16)
    m.negb = sb("negb", [E, P], BF16)
    m.pixb = sb("pixb", [P, 1], BF16)
    m.rt = sb("rt", [P, 9, 2 * E])
    m.rb = sb("rbf", [P, 5, TT, E], BF16)
    m.trb = sb("trb", [E, 8, P], BF16)
    m.oh = sb("oh", [E, NB], BF16)
    m.jm = sb("jm", [E, NOV], BF16)
    m.nbb = sb("nbb", [E, 1], BF16)
    m.col = sb("mcol", [E, 8])
    m.ov = sb("ov", [E, 3, NOV])
    m.tab = sb("tab", [1, NB + 1], I32)
    m.gu_landed = [[c.sem(f"gu_landed{layer}{s}{ab}") for ab in range(2)] for s in range(2)]
    m.dn_landed = [[c.sem(f"dn_landed{layer}{s}{ab}") for ab in range(2)] for s in range(2)]
    m.bc_landed = c.sem(f"bc_landed{layer}")
    return m


def load_block(sp, c, a, m, layer, slot, ab, expert, what):
    buf, src, size, landed = (c.gu, a["gate_up"], GU_PAIR, m.gu_landed) if what == "gu" else (c.dn, a["down"], DN_PAIR, m.dn_landed)
    at = size * slot + size // 2 * ab
    sp.dma_start(buf[:, at:at + size // 2], src[ds(E * layer + expert, 1)].rearrange("e p n -> (e p) n")).then_inc(landed[slot][ab], 16)


def ada_rows(nc, c, a, m):
    done, turned, copied, c.rows_out = c.sem("ada_done"), c.sem("ada_turned"), c.sem("ada_copied"), c.sem("rows_out")
    ada_dve = c.sem("ada_dve")
    cols = c.adac[:, ADA_C:ADA_C + 80]
    with nc.Block() as block:
        @block.vector
        def _(dve):
            ch = Chain(dve, ada_dve)
            ch.link(dve.tensor_tensor(cols, cols, c.vec[:, V_ADAB:V_ADAB + 80], ALU.add))
            ch.link(dve.tensor_tensor(cols, cols, c.vec[:, V_ONE:V_ONE + 80], ALU.add))
            signal(dve, dve.tensor_tensor(cols, cols, c.vec[:, V_MUL:V_MUL + 80], ALU.mult), done, 1)

        @block.tensor
        def _(pe):
            pe.wait_ge(done, 1)
            pe.transpose(c.pt[0:80, 0, 0:P], cols, c.cst[:, C_ID:C_ID + P]).then_inc(turned, 1)

        @block.scalar
        def _(act):
            act.wait_ge(turned, 1)
            act.copy(m.work[0:80, 0:P], c.pt[0:80, 0, 0:P]).then_inc(copied, 1)

        @block.sync
        def _(sp):
            sp.wait_ge(copied, 1)
            sp.dma_start(a["ada_scr"], m.work[0:80, 0:P]).then_inc(c.rows_out, 16)
            sp.wait_ge(c.rows_out, 16)


def bc_row(a, r):
    return a["ada_scr"][KD * r:KD * (r + 1)].rearrange("k p -> (k p)").partition_broadcast(P)


def router(nc, c, a, m, layer):
    pt, pa = c.pt, c.pa
    L = str(layer)
    sem = lambda n: c.sem(n + L)
    w_landed, sgw_landed = sem("rw_landed"), sem("sgw_landed")
    y_in, y_sq, y_ms, y_rt, x_new, x_sq, x_ms, x_rt, h_ready, h_hi, h_lo = (
        sem(n) for n in ("y_in", "y_sq", "y_ms", "y_rt", "x_new", "x_sq", "x_ms", "x_rt", "h_ready", "h_hi", "h_lo"))
    ht_ps, ht_sb, lg_ps, scores, sgu_ps, sgu_act, sact_ready, casts = (
        sem(n) for n in ("ht_ps", "ht_sb", "lg_ps", "scores", "sgu_ps", "sgu_act", "sact_ready", "casts"))
    chosen, cum_ps, parts, tr_ps, tr_sb, oh_ready, tab_ps, shared_done = (
        sem(n) for n in ("chosen", "cum_ps", "parts", "rtr_ps", "rtr_sb", "oh_ready", "tab_ps", "shared_done"))
    r_dve, r_act = sem("r_dve"), sem("r_act")
    ident = c.cst[:, C_ID:C_ID + P]
    hreg = [c.hT[:, 4 * t:4 * t + 4, T:2 * T] for t in range(TT)]
    as4 = lambda ap: ap.rearrange("p (k n) -> p k n", k=4)
    sgw = c.dn[:, DN_PAIR:2 * DN_PAIR].rearrange("p (k n) -> p k n", k=KD)
    sdw = m.work[:].rearrange("p (j n) -> p j n", j=2)
    row = (0, 6)[layer]
    sc, sel, m8, cmp, cmp2, msel, rep, sm, w = (m.rt[:, i, :] for i in range(9))
    per_t = lambda ap: ap.rearrange("p (t e) -> p t e", t=TT)

    with nc.Block() as block:
        @block.sync
        def _(sp):
            for n in range(3):
                sp.dma_start(m.bc[:, n, :], bc_row(a, row + n)).then_inc(m.bc_landed, 16)
            sp.dma_start(m.rw[:].rearrange("p k e -> p (k e)"), a["router_w"][layer]).then_inc(w_landed, 16)
            sp.dma_start(c.dn[:, DN_PAIR:2 * DN_PAIR], a["sh_gate_up"][layer]).then_inc(sgw_landed, 16)
            sp.dma_start(m.work[:], a["sh_down"][layer]).then_inc(sgw_landed, 16)
            for slot in range(2):
                for ab in range(2):
                    load_block(sp, c, a, m, layer, slot, ab, 2 * slot + ab, "gu")
                if slot == 1:
                    sp.wait_ge(sgu_ps, 1)
                for ab in range(2):
                    load_block(sp, c, a, m, layer, slot, ab, 2 * slot + ab, "dn")

        @block.tensor
        def _(pe):
            for n in range(4):
                for k in (2 * n, 2 * n + 1):
                    for t in range(TT):
                        if n == 0:
                            pe.wait_ge(h_ready, t + 1)
                            if t == 0:
                                pe.wait_ge(x_sq, 2)
                        mm = pe.transpose(pt[:, n, T * (k % 2) + P * t:T * (k % 2) + P * (t + 1)],
                                          hreg[t][:, k // 2, P * (k % 2):P * (k % 2 + 1)], ident)
                mm.then_inc(ht_ps, 1)
            pe.wait_ge(w_landed, 16)
            pe.wait_ge(ht_sb, 4)
            for t in range(TT):
                for k in range(KD):
                    mm = pe.matmul(pt[:, 0, E * t:E * (t + 1)], c.hT[:, k, P * t:P * (t + 1)], m.rw[:, k, :], start=k == 0, stop=k == KD - 1)
            mm.then_inc(lg_ps, 1)
            pe.wait_ge(sgw_landed, 32)
            for j in range(4):
                for k in range(KD):
                    mm = pe.matmul(pt[:, 1 + j // 2, T * (j % 2):T * (j % 2 + 1)], sgw[:, k, P * j:P * (j + 1)], c.hT[:, k, 0:T], start=k == 0, stop=k == KD - 1)
            mm.then_inc(sgu_ps, 1)
            pe.wait_ge(chosen, 1)
            cb = m.rb[:, 0]
            pe.matmul(pt[:, 3, 0:E], m.tub[:], cb[:, 0, :], start=True, stop=True)
            pe.matmul(pt[:, 3, E:2 * E], m.tub[:], cb[:, 1, :], start=True, stop=False)
            pe.matmul(pt[:, 3, E:2 * E], m.oneb[:], cb[:, 0, :], start=False, stop=True)
            for t in range(TT):
                mm = pe.matmul(pt[0:E, 3, 2 * E:2 * E + 1], cb[:, t, :], m.oneb[:, 0:1], start=t == 0, stop=t == TT - 1)
            mm.then_inc(cum_ps, 1)
            pe.wait_ge(sact_ready, 1)
            for t in range(TT):
                for h in range(2):
                    for j in range(2):
                        mm = pe.matmul(pa[:, 2 * t + h, :], m.actT[:, j, P * t:P * (t + 1)], sdw[:, j, 512 * h:512 * (h + 1)], start=j == 0, stop=False, skip_group_check=True)
            mm.then_inc(shared_done, 1)
            pe.wait_ge(parts, 1)
            turned = pt[0:E, 0, :].bitcast(BF16)
            for n in range(4):
                for t in range(TT):
                    pe.transpose(turned[:, P * (2 * n + t):P * (2 * n + t + 1)], m.rb[:, 1 + n, t, :], m.idb[:])
            pe.matmul(pt[0:E, 3, 130:131], m.tub[0:E, 0:E], m.nbb[:], start=True, stop=True).then_inc(tr_ps, 1)
            pe.wait_ge(tr_sb, 1)
            pe.wait_ge(oh_ready, 1)
            for t in range(TT):
                pe.matmul(pt[:, 1, NB * t:NB * (t + 1)], m.trb[:, t, :], m.oh[:], start=True, stop=False, skip_group_check=True)
                pe.matmul(pt[:, 1, NB * t + E:NB * (t + 1)], m.negb[:], m.jm[:], start=False, stop=True, skip_group_check=True)
            for n in range(3):
                for t in range(TT):
                    pe.matmul(pt[:, 2, NB * n:NB * (n + 1)] if t == 0 else pt[:, 0, NB * n:NB * (n + 1)], m.trb[:, 2 + 2 * n + t, :], m.oh[:], start=True, stop=True)
            pe.matmul(pt[0:1, 3, 140:140 + NOV], m.pixb[0:E, :], m.oh[:, E:NB], start=True, stop=True)
            pe.matmul(pt[0:1, 3, 140 + NOV:141 + NOV], m.nbb[:], m.oneb[0:E, 0:1], start=True, stop=True).then_inc(tab_ps, 1)

        @block.scalar
        def _(act):
            ch = Chain(act, r_act)
            for t in range(TT):
                act.wait_ge(y_in, t + 1)
                signal(act, act.activation(as4(pt[:, 2 * t:2 * t + 2, :].rearrange("p b n -> p (b n)")), hreg[t], ACT.Square, accum_out=m.nrm[:, t:t + 1]), y_sq, t + 1)
            act.wait_ge(y_ms, 1)
            signal(act, act.activation(m.nrm[:, 4:6], m.nrm[:, 2:4], ACT.Sqrt), y_rt, 1)
            for t in range(TT):
                act.wait_ge(x_new, t + 1)
                signal(act, act.activation(pt[:, 2 * t:2 * t + 2, :].rearrange("p b n -> p (b n)"), c.x[:, t, :], ACT.Square, accum_out=m.nrm[:, 8 + t:9 + t]), x_sq, t + 1)
            act.wait_ge(x_ms, 1)
            signal(act, act.activation(m.nrm[:, 12:14], m.nrm[:, 10:12], ACT.Sqrt), x_rt, 1)
            for t in range(TT):
                act.wait_ge(h_ready, t + 1)
                signal(act, act.copy(as4(m.hr[:, 0, t, :]), hreg[t]), h_hi, t + 1)
            for n in range(4):
                act.wait_ge(ht_ps, n + 1)
                signal(act, act.copy(c.hT[:, 2 * n:2 * n + 2, 0:T], pt[:, n, :].rearrange("p (k n) -> p k n", k=2)), ht_sb, n + 1)
            act.wait_ge(lg_ps, 1)
            signal(act, act.activation(sc, pt[:, 0, 0:2 * E], ACT.Sigmoid), scores, 1)
            act.wait_ge(sgu_ps, 1)
            signal(act, act.activation(m.sg[:], pt[:, 1, :], ACT.Silu), sgu_act, 1)
            act.wait_ge(tr_ps, 1)
            signal(act, act.copy(m.trb[:].rearrange("p n t -> p (n t)"), pt[0:E, 0, :].bitcast(BF16)), tr_sb, 1)

        @block.vector
        def _(dve):
            ch = Chain(dve, r_dve)
            if layer == 1:
                dve.wait_ge(c.const_landed, 64)
            for t in range(TT):
                src = as4(pa[:, 2 * t:2 * t + 2, :].rearrange("p b n -> p (b n)"))
                if layer == 0:
                    ins = dve.tensor_copy(hreg[t], src)
                else:
                    ins = dve.tensor_tensor(hreg[t], src, as4(c.rows[:, R_BO:R_BO + D]), ALU.add)
                signal(dve, ins, y_in, t + 1)
            for out, src in ((m.idb, C_ID), (m.tub, C_TU), (m.oneb, C_ONE)):
                ch.post(dve.tensor_copy(out[:], c.cst[:, src:src + P]))
            ch.post(dve.tensor_copy(m.pixb[:], c.cst[:, C_PIX:C_PIX + 1]))
            ch.post(dve.memset(m.negb[:], -float(CAP)))
            ch.post(dve.tensor_copy(m.oh[:, 0:E], c.cst[0:E, C_ID:C_ID + E]))
            ch.post(dve.tensor_copy(m.tab[:, 0:E], c.cst[0:1, C_IE:C_IE + E]))
            ch.link(dve.memset(m.st[:].bitcast(F32), 0.0))
            dve.wait_ge(y_sq, 2)
            signal(dve, dve.tensor_scalar(m.nrm[:, 2:4], m.nrm[:, 0:2], 1.0 / D, EPS, ALU.mult, ALU.add), y_ms, 1)
            dve.wait_ge(y_rt, 1)
            ch.link(dve.reciprocal(m.nrm[:, 6:8], m.nrm[:, 4:6]))
            dve.wait_ge(m.bc_landed, 48)
            for t in range(TT):
                ch.link(dve.scalar_tensor_tensor(out=hreg[t], in0=hreg[t], scalar=m.nrm[:, 6 + t:7 + t], in1=as4(m.bc[:, 0, :]), op0=ALU.mult, op1=ALU.mult))
                signal(dve, dve.tensor_tensor(as4(c.x[:, t, :]), as4(c.x[:, t, :]), hreg[t], ALU.add), x_new, t + 1)
            dve.wait_ge(x_sq, 2)
            signal(dve, dve.tensor_scalar(m.nrm[:, 10:12], m.nrm[:, 8:10], 1.0 / D, EPS, ALU.mult, ALU.add), x_ms, 1)
            dve.wait_ge(x_rt, 1)
            ch.link(dve.reciprocal(m.nrm[:, 14:16], m.nrm[:, 12:14]))
            for t in range(TT):
                ch.link(dve.scalar_tensor_tensor(out=hreg[t], in0=as4(c.x[:, t, :]), scalar=m.nrm[:, 14 + t:15 + t], in1=as4(m.bc[:, 1, :]), op0=ALU.mult, op1=ALU.mult))
                signal(dve, dve.tensor_tensor(hreg[t], hreg[t], as4(m.bc[:, 2, :]), ALU.add), h_ready, t + 1)
            for t in range(TT):
                dve.wait_ge(h_hi, t + 1)
                signal(dve, dve.tensor_tensor(as4(m.hr[:, 1, t, :]), hreg[t], as4(m.hr[:, 0, t, :].bitcast(F32)), ALU.subtract), h_lo, t + 1)
            dve.wait_ge(scores, 1)
            rb = c.rows[:, R_RB + E * layer:R_RB + E * (layer + 1)].unsqueeze(1).broadcast_to([P, TT, E])
            ch.link(dve.tensor_tensor(per_t(sel), per_t(sc), rb, ALU.add))
            for n in range(2 * G):
                ins = dve.max(m8[:, 8 * n:8 * n + 8], sel[:, 8 * n:8 * n + 8])
                ch.post(ins) if n < 2 * G - 1 else ch.link(ins)
            best = m8.rearrange("p (n j) -> p n j", j=8)
            gs = msel[:, 0:16]
            ch.link(dve.tensor_tensor(gs.unsqueeze(2), best[:, :, 0:1], best[:, :, 1:2], ALU.add))
            gst = gs.rearrange("p (t g) -> p t g", t=TT)
            other, own = gst.unsqueeze(2).broadcast_to([P, TT, 8, 8]), gst.unsqueeze(3).broadcast_to([P, TT, 8, 8])
            four = lambda ap: ap.rearrange("p (t g j) -> p t g j", t=TT, g=8)
            before = c.cst[:, C_LT8:C_LT8 + 64].rearrange("p (g j) -> p g j", g=8).unsqueeze(1).broadcast_to([P, TT, 8, 8])
            ch.post(dve.tensor_tensor(four(cmp), other, own, ALU.is_gt))
            ch.link(dve.tensor_tensor(four(cmp2), other, own, ALU.is_equal))
            ch.link(dve.tensor_tensor(four(cmp2), four(cmp2), before, ALU.mult))
            ch.link(dve.tensor_tensor(cmp, cmp, cmp2, ALU.add))
            ch.link(dve.tensor_reduce(rep[:, 0:16], cmp.rearrange("p (n j) -> p n j", j=8), AX.X, ALU.add))
            ch.link(dve.tensor_scalar(rep[:, 16:32], rep[:, 0:16], 3.5, None, ALU.is_lt))
            ch.link(dve.tensor_scalar(rep[:, 32:48], rep[:, 16:32], 1.0, BIG, ALU.subtract, ALU.mult))
            eight = lambda ap: ap.rearrange("p (n j) -> p n j", j=8)
            over8 = lambda ap: ap.unsqueeze(2).broadcast_to([P, 16, 8])
            ch.link(dve.tensor_tensor(eight(msel), eight(sel), over8(rep[:, 16:32]), ALU.mult))
            ch.link(dve.tensor_tensor(eight(msel), eight(msel), over8(rep[:, 32:48]), ALU.add))
            for t in range(TT):
                ch.link(dve.max(m8[:, 8 * t:8 * t + 8], msel[:, E * t:E * (t + 1)]))
            for t in range(TT):
                ch.link(dve.match_replace(rep[:, E * t:E * (t + 1)], m8[:, 8 * t:8 * t + 8], msel[:, E * t:E * (t + 1)], -3e38))
            ch.link(dve.tensor_scalar(sm, rep, -2.0 * BIG, None, ALU.is_lt))
            signal(dve, dve.tensor_copy(m.rb[:, 0], per_t(sm)), chosen, 1)
            ch.link(dve.tensor_tensor(w, sc, sm, ALU.mult))
            ch.link(dve.tensor_reduce(m.nrm[:, 0:2], per_t(w), AX.X, ALU.add))
            ch.link(dve.reciprocal(m.nrm[:, 2:4], m.nrm[:, 0:2]))
            for t in range(TT):
                ch.link(dve.tensor_scalar(w[:, E * t:E * (t + 1)], w[:, E * t:E * (t + 1)], m.nrm[:, 2 + t:3 + t], 2.5, ALU.mult, ALU.mult))
            for n in range(2):
                ch.link(dve.tensor_copy(m.rb[:, 2 + n], per_t(w)))
                ch.link(dve.tensor_tensor(per_t(w), per_t(w), m.rb[:, 2 + n], ALU.subtract))
            ch.link(dve.tensor_copy(m.rb[:, 4], per_t(w)))
            dve.wait_ge(cum_ps, 1)
            ch.link(dve.tensor_tensor(m.rb[:, 1], per_t(pt[:, 3, 0:2 * E]), per_t(sm), ALU.mult))
            cnt = pt[0:E, 3, 2 * E:2 * E + 1]
            ch.link(dve.tensor_copy(m.col[:, 0:1], cnt))
            ch.link(dve.tensor_scalar(m.col[:, 1:2], m.col[:, 0:1], float(CAP), None, ALU.is_gt))
            for n in (2, 3):
                ch.link(dve.scalar_tensor_tensor(out=m.col[:, n:n + 1], in0=m.col[:, 0:1], scalar=float(n * CAP), in1=m.col[:, n - 1:n], op0=ALU.is_gt, op1=ALU.add))
            signal(dve, dve.tensor_copy(m.nbb[:], m.col[:, 3:4]), parts, 1)
            dve.wait_ge(sgu_act, 1)
            signal(dve, dve.tensor_tensor(m.actT[:].rearrange("p j t -> p (j t)"), pt[:, 2, :], m.sg[:], ALU.mult), sact_ready, 1)
            dve.wait_ge(tr_ps, 1)
            ch.link(dve.tensor_copy(m.col[:, 4:5], pt[0:E, 3, 130:131]))
            ch.link(dve.tensor_tensor(m.col[:, 5:6], m.col[:, 4:5], m.col[:, 3:4], ALU.subtract))
            iov = c.cst[0:E, C_IOV:C_IOV + NOV]
            ch.post(dve.tensor_scalar(m.ov[:, 0, :], iov, m.col[:, 5:6], None, ALU.is_ge))
            ch.link(dve.tensor_scalar(m.ov[:, 1, :], iov, m.col[:, 4:5], None, ALU.is_ge))
            ch.link(dve.tensor_tensor(m.ov[:, 0, :], m.ov[:, 0, :], m.ov[:, 1, :], ALU.subtract))
            ch.link(dve.tensor_copy(m.oh[:, E:NB], m.ov[:, 0, :]))
            ch.link(dve.tensor_scalar(m.ov[:, 2, :], iov, m.col[:, 5:6], 1.0, ALU.subtract, ALU.add))
            signal(dve, dve.tensor_tensor(m.jm[:], m.ov[:, 0, :], m.ov[:, 2, :], ALU.mult), oh_ready, 1)
            dve.wait_ge(tab_ps, 1)
            for t in range(TT):
                ch.post(dve.tensor_scalar(m.rk[:, :, t, :], pt[:, 1, NB * t:NB * (t + 1)].rearrange("p (n b) -> p n b", b=2), 1.0, None, ALU.subtract))
                for n in range(3):
                    ch.post(dve.tensor_copy(m.wb[:, :, t, n, :], pt[:, 2 if t == 0 else 0, NB * n:NB * (n + 1)].rearrange("p (n b) -> p n b", b=2)))
            ch.link(dve.tensor_copy(m.tab[:, E:NB + 1], pt[0:1, 3, 140:141 + NOV]))


def own_place(dve, c, m, out, pair):
    places = c.cst[:, C_I64:C_I64 + CAP].unsqueeze(1).broadcast_to([P, 2 * TT, CAP])
    rank = m.rk[:, ds(pair, 1), :, :].rearrange("p n t b -> p (n t b)").unsqueeze(2).broadcast_to([P, 2 * TT, CAP])
    return dve.tensor_tensor(out[:].rearrange("p t (b s) -> p (t b) s", b=2), places, rank, ALU.is_equal)


def experts(nc, c, a, m, layer):
    pt, pa = c.pt, c.pa
    L = str(layer)
    sem = lambda n: c.sem(n + L)
    s_ready, sb_ready = sem("s_ready"), sem("sb_ready")
    x_ps, x_sb, xt_ps, xt_act, xt_dve = (sem(n) for n in ("x_ps", "x_sb", "ext_ps", "ext_act", "ext_dve"))
    gu_ps, silu_done, slot_ps, wsl_ready, st_sb, act_ready = (sem(n) for n in ("gu_ps", "silu_done", "slot_ps", "wsl_ready", "st_sb", "act_ready"))
    at_ps, at_sb, y_ps, y_hi, y_lo, scat = (sem(n) for n in ("at_ps", "at_sb", "ey_ps", "y_hi", "y_lo", "scat"))
    e_dve = sem("e_dve")
    ident = c.cst[:, C_ID:C_ID + P]
    X = m.work[:, 0:D]
    XT = m.work[:, D:2 * D].rearrange("p (k s) -> p k s", k=KD)
    scaled = m.actT[:, :, 0:P]

    def quads(eng):
        nov = eng.value_load(m.tab[0:1, NB:NB + 1], min_val=0, max_val=31)
        return E // 4 + (nov + 3) // 4

    with nc.Block() as block:
        @block.sync
        def _(sp):
            sp.dma_start(m.bc[:, 0, :], bc_row(a, (3, 9)[layer])).then_inc(m.bc_landed, 16)
            n = quads(sp)
            with sp.Fori(1, n) as i:
                for slot in range(2):
                    pair = 2 * i + slot
                    e = [sp.value_load(m.tab[0:1, ds(2 * pair + ab, 1)], min_val=0, max_val=E - 1) for ab in range(2)]
                    sp.wait_ge(gu_ps, pair - 1)
                    for ab in range(2):
                        load_block(sp, c, a, m, layer, slot, ab, e[ab], "gu")
                    sp.wait_ge(y_ps, 2 * (pair - 1))
                    for ab in range(2):
                        load_block(sp, c, a, m, layer, slot, ab, e[ab], "dn")

        @block.tensor
        def _(pe):
            def gather(pair):
                pe.wait_ge(s_ready, pair + 1)
                for h in range(2):
                    for part in range(2):
                        for t in range(TT):
                            mm = pe.matmul(pt[:, 1 + h, :], m.sr[:, t, :], m.hr[:, part, t, 512 * h:512 * (h + 1)],
                                           start=part + t == 0, stop=part + t == 2)
                    mm.then_inc(x_ps, 1)

            def turn(pair):
                pe.wait_ge(x_sb, 2 * pair + 2)
                for k in range(KD):
                    mm = pe.transpose(pt[:, 1 + k // 4, P * (k % 4):P * (k % 4 + 1)], X[:, P * k:P * (k + 1)], ident)
                    if k % 4 == 3:
                        mm.then_inc(xt_ps, 1)

            def scatter():
                for t in range(TT):
                    for h in range(2):
                        for part in range(2):
                            mm = pe.matmul(pa[:, 2 * t + h, :], m.st[:, P * t:P * (t + 1)], m.ys[:, part, 512 * h:512 * (h + 1)],
                                           start=False, stop=False, skip_group_check=True)
                mm.then_inc(scat, 1)

            def body(pair, slot, i):
                pe.wait_ge(xt_act, pair + 1)
                pe.wait_ge(xt_dve, pair + 1)
                pe.wait_ge(y_lo, 2 * pair + 2)
                for ab in range(2):
                    pe.wait_ge(m.gu_landed[slot][ab], 16 * i + 16)
                for k in range(KD):
                    for ab in range(2):
                        at = GU_PAIR * slot + GU_PAIR // 2 * ab + 512 * k
                        mm = pe.matmul(pt[CAP * ab:CAP * (ab + 1), 0, :], XT[:, k, CAP * ab:CAP * (ab + 1)], c.gu[:, at:at + 512],
                                       start=k == 0, stop=k == KD - 1)
                mm.then_inc(gu_ps, 1)
                scatter()
                pe.wait_ge(sb_ready, pair + 1)
                for t in range(TT):
                    pe.matmul(pt[:, 3, T:T + 6], m.sb[:, t, :], m.wb[:, ds(pair, 1), t, :, :].rearrange("p n a b -> p (n a b)"), start=t == 0, stop=t == TT - 1)
                st = pt[:, 3, 0:P].bitcast(BF16)
                for t in range(TT):
                    mm = pe.transpose(st[:, P * t:P * (t + 1)], m.sb[:, t, :], m.idb[:])
                mm.then_inc(slot_ps, 1)
                gather(pair + 1)
                pe.wait_ge(st_sb, pair + 1)
                pe.wait_ge(act_ready, pair + 1)
                for j in range(2):
                    mm = pe.transpose(pt[:, 3, P * j:P * (j + 1)], m.act[:, P * j:P * (j + 1)], ident)
                mm.then_inc(at_ps, 1)
                turn(pair + 1)
                pe.wait_ge(at_sb, pair + 1)
                for ab in range(2):
                    pe.wait_ge(m.dn_landed[slot][ab], 16 * i + 16)
                for h in range(2):
                    for j in range(2):
                        for ab in range(2):
                            at = DN_PAIR * slot + DN_PAIR // 2 * ab + D * j + 512 * h
                            mm = pe.matmul(pt[CAP * ab:CAP * (ab + 1), 3 * h, :], scaled[:, j, CAP * ab:CAP * (ab + 1)], c.dn[:, at:at + 512],
                                           start=j == 0, stop=j == 1)
                    mm.then_inc(y_ps, 1)

            n = quads(pe)
            gather(0)
            turn(0)
            with pe.Fori(0, n) as i:
                for slot in range(2):
                    body(2 * i + slot, slot, i)
            pe.wait_ge(y_lo, 4 * n + 2)
            scatter()

        @block.scalar
        def _(act):
            def take(pair):
                for h in range(2):
                    act.wait_ge(x_ps, 2 * pair + h + 1)
                    signal(act, act.copy(X[:, 512 * h:512 * (h + 1)], pt[:, 1 + h, :]), x_sb, 2 * pair + h + 1)

            def take_turned(pair):
                act.wait_ge(xt_ps, 2 * pair + 1)
                signal(act, act.copy(XT[:, 0:4, :].rearrange("p k s -> p (k s)"), pt[:, 1, :]), xt_act, pair + 1)

            def body(pair):
                act.wait_ge(gu_ps, pair + 1)
                signal(act, act.activation(m.sg[:, 0:F], pt[:, 0, 0:F], ACT.Silu), silu_done, pair + 1)
                take(pair + 1)
                act.wait_ge(at_ps, pair + 1)
                signal(act, act.copy(scaled, pt[:, 3, 0:T].rearrange("p (j s) -> p j s", j=2)), at_sb, pair + 1)
                take_turned(pair + 1)
                for h in range(2):
                    act.wait_ge(y_ps, 2 * pair + h + 1)
                    signal(act, act.copy(m.ys[:, 0, 512 * h:512 * (h + 1)], pt[:, 3 * h, :]), y_hi, 2 * pair + h + 1)

            n = quads(act)
            take(0)
            take_turned(0)
            with act.Fori(0, n) as i:
                for slot in range(2):
                    body(2 * i + slot)

        @block.vector
        def _(dve):
            ch = Chain(dve, e_dve)

            def take_turned(pair):
                dve.wait_ge(xt_ps, 2 * pair + 2)
                signal(dve, dve.tensor_copy(XT[:, 4:8, :].rearrange("p k s -> p (k s)"), pt[:, 2, :]), xt_dve, pair + 1)

            def body(pair):
                dve.wait_ge(x_ps, 2 * pair + 2)
                signal(dve, own_place(dve, c, m, m.sr, pair + 1), s_ready, pair + 2)
                dve.wait_ge(slot_ps, pair + 1)
                parts = pt[:, 3, T:T + 6].rearrange("p (n b) -> p b n", b=2)
                for ab in range(2):
                    half = slice(CAP * ab, CAP * (ab + 1))
                    ins = dve.tensor_reduce(m.wsl[half, :], parts[half, ab, :], AX.X, ALU.add)
                    ch.post(ins) if ab == 0 else ch.link(ins)
                signal(dve, dve.tensor_copy(m.st[:], pt[:, 3, 0:P].bitcast(BF16)), st_sb, pair + 1)
                dve.wait_ge(silu_done, pair + 1)
                signal(dve, dve.scalar_tensor_tensor(out=m.act[:], in0=pt[:, 0, F:2 * F], scalar=m.wsl[:], in1=m.sg[:, 0:F], op0=ALU.mult, op1=ALU.mult), act_ready, pair + 1)
                signal(dve, own_place(dve, c, m, m.sb, pair + 1), sb_ready, pair + 2)
                take_turned(pair + 1)
                for h in range(2):
                    dve.wait_ge(y_hi, 2 * pair + h + 1)
                    cols = slice(512 * h, 512 * (h + 1))
                    signal(dve, dve.tensor_tensor(m.ys[:, 1, cols], pt[:, 3 * h, :], m.ys[:, 0, cols].bitcast(F32), ALU.subtract), y_lo, 2 * pair + h + 3)

            signal(dve, own_place(dve, c, m, m.sr, 0), s_ready, 1)
            for part in range(2):
                signal(dve, dve.memset(m.ys[:, part, :].bitcast(F32), 0.0), y_lo, part + 1)
            signal(dve, own_place(dve, c, m, m.sb, 0), sb_ready, 1)
            n = quads(dve)
            take_turned(0)
            with dve.Fori(0, n) as i:
                for slot in range(2):
                    ch.at(4 * i + 2 * slot)
                    body(2 * i + slot)


def ffn_end(nc, c, a, m, layer):
    pt, pa = c.pt, c.pa
    L = str(layer)
    f_sq, f_ms, f_rt, f_x, out_done = (c.sem(n + L) for n in ("f_sq", "f_ms", "f_rt", "f_x", "out_done"))
    f_dve = c.sem("f_dve" + L)
    flat = lambda t: pa[:, 2 * t:2 * t + 2, :].rearrange("p b n -> p (b n)")
    with nc.Block() as block:
        @block.scalar
        def _(act):
            for t in range(TT):
                signal(act, act.activation(pt[:, 2 * t:2 * t + 2, :].rearrange("p b n -> p (b n)"), flat(t), ACT.Square, accum_out=m.nrm[:, t:t + 1]), f_sq, t + 1)
            act.wait_ge(f_ms, 1)
            signal(act, act.activation(m.nrm[:, 4:6], m.nrm[:, 2:4], ACT.Sqrt), f_rt, 1)

        @block.vector
        def _(dve):
            ch = Chain(dve, f_dve)
            dve.wait_ge(f_sq, 2)
            signal(dve, dve.tensor_scalar(m.nrm[:, 2:4], m.nrm[:, 0:2], 1.0 / D, EPS, ALU.mult, ALU.add), f_ms, 1)
            dve.wait_ge(f_rt, 1)
            ch.link(dve.reciprocal(m.nrm[:, 6:8], m.nrm[:, 4:6]))
            dve.wait_ge(m.bc_landed, 64)
            for t in range(TT):
                ch.link(dve.scalar_tensor_tensor(out=m.work[:, 0:D], in0=flat(t), scalar=m.nrm[:, 6 + t:7 + t], in1=m.bc[:, 0, :], op0=ALU.mult, op1=ALU.mult))
                signal(dve, dve.tensor_tensor(c.x[:, t, :], c.x[:, t, :], m.work[:, 0:D], ALU.add), f_x, t + 1)

        if layer == 1:
            @block.sync
            def _(sp):
                for t in range(TT):
                    sp.wait_ge(f_x, t + 1)
                    sp.dma_start(a["out"][t], c.x[:, t, :]).then_inc(out_done, 16)
                sp.wait_ge(out_done, 32)



def conformer(nc, c, a, s):
    pt, pa = c.pt, c.pa
    xn = c.sb("cxn", [P, TT, D], F32, s)
    u = c.sb("cu", [P, KD, NROW, PADROW], F32, s)
    v = c.sb("cvs", [P, KD, T], F32, s)
    sq = c.sb("csq", [P, KD, T], F32, s)
    rstd = c.sb("crstd", [P, T], F32, s)
    nrm = c.sb("cnrm", [P, 8], F32, s)
    in_landed = [c.sem(f"cvin_landed{j}") for j in range(KD)]
    out_landed = c.sem("cvout_landed")
    x_sq, x_ms, x_rt, xn_ready, xt_ps, h_sb = (c.sem(n) for n in ("cx_sq", "cx_ms", "cx_rt", "cxn_ready", "cxt_ps", "ch_sb"))
    glu_ps, gate_done, u_ready, v_ready, mu_ps, xc_ready, sq_ready, var_ps, var_e, std, ln_ready, sw, co_ps = (
        c.sem(n) for n in ("glu_ps", "gate_done", "u_ready", "v_ready", "mu_ps", "xc_ready", "sq_ready", "var_ps", "var_e", "std", "ln_ready", "swish", "co_ps"))
    c_dve, c_act = c.sem("c_dve"), c.sem("c_act")
    sigm = sq
    ident = c.cst[:, C_ID:C_ID + P]
    ones = c.cst[:, C_ONE:C_ONE + P]
    shift = c.adac[:, ADA_C + 4 * KD:ADA_C + 5 * KD]
    scale = c.adac[:, ADA_C + 5 * KD:ADA_C + 6 * KD]
    win = [c.gu[:, 2048 * j:2048 * (j + 1)].rearrange("p (k n) -> p k n", k=KD) for j in range(KD)]
    wout = c.dn[:].rearrange("p (k n) -> p k n", k=KD)
    pair = lambda n: pt[:, 2 * n:2 * n + 2, :].rearrange("p b n -> p (b n)")

    with nc.Block() as block:
        @block.sync
        def _(sp):
            for j in range(KD):
                sp.dma_start(c.gu[:, 2048 * j:2048 * (j + 1)], a["cv_in"][j]).then_inc(in_landed[j], 16)
            sp.dma_start(c.dn[:], a["cv_out"]).then_inc(out_landed, 16)

        @block.tensor
        def _(pe):
            pe.wait_ge(x_sq, 2)
            for n in range(4):
                for k in (2 * n, 2 * n + 1):
                    for t in range(TT):
                        if n == 0:
                            pe.wait_ge(xn_ready, t + 1)
                        mm = pe.transpose(pt[:, n, T * (k % 2) + P * t:T * (k % 2) + P * (t + 1)], xn[:, t, P * k:P * (k + 1)], ident)
                mm.then_inc(xt_ps, 1)
            pe.wait_ge(h_sb, KD)
            for j in range(KD):
                pe.wait_ge(in_landed[j], 16)
                if j >= 2:
                    pe.wait_ge(u_ready, j - 1)
                for half in range(2):
                    for k in range(KD):
                        mm = pe.matmul(pt[:, 2 * (j % 2) + half, 0:T], win[j][:, k, P * half:P * (half + 1)], c.hT[:, k, 0:T], start=k == 0, stop=k == KD - 1)
                mm.then_inc(glu_ps, 1)
            for k in range(KD):
                pe.wait_ge(v_ready, k + 1)
                mm = pe.matmul(pa[:, 0, 0:T], ones, v[:, k, :], start=k == 0, stop=k == KD - 1)
            mm.then_inc(mu_ps, 1)
            pe.wait_ge(sq_ready, 1)
            for k in range(KD):
                mm = pe.matmul(pa[:, 1, 0:T], ones, sq[:, k, :], start=k == 0, stop=k == KD - 1)
            mm.then_inc(var_ps, 1)
            pe.wait_ge(out_landed, 16)
            for k in range(KD):
                pe.wait_ge(sw, k + 1)
                for t in range(TT):
                    for h in range(2):
                        mm = pe.matmul(pa[:, 2 * t + h, :], v[:, k, P * t:P * (t + 1)], wout[:, k, 512 * h:512 * (h + 1)], start=k == 0, stop=k == KD - 1, skip_group_check=True)
            mm.then_inc(co_ps, 1)

        @block.scalar
        def _(act):
            for t in range(TT):
                signal(act, act.activation(pair(t), c.x[:, t, :], ACT.Square, accum_out=nrm[:, t:t + 1]), x_sq, t + 1)
            act.wait_ge(x_ms, 1)
            signal(act, act.activation(nrm[:, 4:6], nrm[:, 2:4], ACT.Sqrt), x_rt, 1)
            for k in range(KD):
                act.wait_ge(xt_ps, k // 2 + 1)
                signal(act, act.activation(c.hT[:, k, 0:T], pt[:, k // 2, T * (k % 2):T * (k % 2 + 1)], ACT.Identity,
                                           bias=shift[:, k:k + 1], scale=scale[:, k:k + 1]), h_sb, k + 1)
            for j in range(KD):
                act.wait_ge(glu_ps, j + 1)
                signal(act, act.activation(sigm[:, j, :], pt[:, 2 * (j % 2) + 1, 0:T], ACT.Sigmoid, bias=c.vec[:, V_CBI + KD + j:V_CBI + KD + j + 1]), gate_done, j + 1)
            act.wait_ge(xc_ready, 1)
            signal(act, act.activation(sq[:].rearrange("p k t -> p (k t)"), v[:].rearrange("p k t -> p (k t)"), ACT.Square), sq_ready, 1)
            act.wait_ge(var_e, 1)
            signal(act, act.activation(rstd[:], rstd[:], ACT.Sqrt), std, 1)
            for k in range(KD):
                act.wait_ge(ln_ready, k + 1)
                signal(act, act.activation(v[:, k, :], v[:, k, :], ACT.Silu, bias=c.vec[:, V_LNB + k:V_LNB + k + 1], scale=c.vec[:, V_LNG + k:V_LNG + k + 1]), sw, k + 1)

        @block.vector
        def _(dve):
            ch = Chain(dve, c_dve)
            ch.link(dve.memset(u[:], 0.0))
            dve.wait_ge(x_sq, 2)
            signal(dve, dve.tensor_scalar(nrm[:, 2:4], nrm[:, 0:2], 1.0 / D, EPS, ALU.mult, ALU.add), x_ms, 1)
            dve.wait_ge(x_rt, 1)
            ch.link(dve.reciprocal(nrm[:, 6:8], nrm[:, 4:6]))
            for t in range(TT):
                signal(dve, dve.tensor_scalar(xn[:, t, :], c.x[:, t, :], nrm[:, 6 + t:7 + t], None, ALU.mult), xn_ready, t + 1)
            rows = lambda ap: ap.rearrange("p (r l) -> p r l", r=NROW)
            for j in range(KD):
                dve.wait_ge(gate_done, j + 1)
                signal(dve, dve.scalar_tensor_tensor(out=u[:, j, :, TAP31 // 2:TAP31 // 2 + ROW], in0=rows(pt[:, 2 * (j % 2), 0:T]), scalar=c.vec[:, V_CBI + j:V_CBI + j + 1],
                                                     in1=rows(sigm[:, j, :]), op0=ALU.add, op1=ALU.mult), u_ready, j + 1)
                w = lambda tap: c.vec[:, V_DW + TAP31 * j + tap:V_DW + TAP31 * j + tap + 1]
                ch.link(dve.tensor_scalar(rows(v[:, j, :]), u[:, j, :, 0:ROW], w(0), c.vec[:, V_DWB + j:V_DWB + j + 1], ALU.mult, ALU.add))
                for tap in range(1, TAP31):
                    ins = dve.scalar_tensor_tensor(out=rows(v[:, j, :]), in0=u[:, j, :, tap:tap + ROW], scalar=w(tap), in1=rows(v[:, j, :]), op0=ALU.mult, op1=ALU.add)
                    if tap < TAP31 - 1:
                        ch.link(ins)
                signal(dve, ins, v_ready, j + 1)
            over = lambda ap: ap.unsqueeze(1).broadcast_to([P, KD, T])
            dve.wait_ge(mu_ps, 1)
            ch.link(dve.tensor_scalar(rstd[:], pa[:, 0, 0:T], 1.0 / D, None, ALU.mult))
            signal(dve, dve.tensor_tensor(v[:], v[:], over(rstd[:]), ALU.subtract), xc_ready, 1)
            dve.wait_ge(var_ps, 1)
            signal(dve, dve.tensor_scalar(rstd[:], pa[:, 1, 0:T], 1.0 / D, EPS, ALU.mult, ALU.add), var_e, 1)
            dve.wait_ge(std, 1)
            ch.link(dve.reciprocal(rstd[:], rstd[:]))
            for k in range(KD):
                signal(dve, dve.tensor_tensor(v[:, k, :], v[:, k, :], rstd[:], ALU.mult), ln_ready, k + 1)



def constants():
    i = np.arange(P)
    cst = np.zeros((P, C_N), np.float32)
    cst[:, C_ID:C_ID + P] = np.eye(P)
    cst[:, C_TU:C_TU + P] = i[:, None] <= i[None, :]
    cst[:, C_TL:C_TL + P] = i[:, None] >= i[None, :]
    cst[:, C_ONE:C_ONE + P] = 1.0
    cst[:, C_MF:C_MF + P] = np.where(i[:, None] <= i[None, :], 0.0, -BIG)
    cst[:, C_MB:C_MB + P] = np.where(i[:, None] >= i[None, :], 0.0, -BIG)
    cst[:, C_I64:C_I64 + CAP] = np.arange(CAP)
    cst[:, C_IOV:C_IOV + NOV] = np.arange(NOV)
    cst[:, C_LT8:C_LT8 + 64] = (np.arange(8)[None, :] < np.arange(8)[:, None]).reshape(-1)
    cst[:, C_PIX] = i
    cst[:, C_IE:C_IE + E] = np.arange(E)
    return cst


def chunked(v):
    return np.asarray(v).reshape(-1, P).T


def k_major(w):
    k, n = w.shape
    return w.reshape(k // P, P, n).transpose(1, 0, 2).reshape(P, -1)


def layout(i):
    ada_w, ada_b = i["ada_w"], i["ada_b"]
    part = lambda arr, l, n: arr[l][..., n * D:(n + 1) * D]
    order = [(0, 2, i["norm_mix_post"][0], 0), (0, 4, i["norm_ffn_pre"][0], 1), (0, 3, None, 0), (0, 5, i["norm_ffn_post"][0], 0),
             (1, 0, None, 0), (1, 1, i["norm_mix_pre"][1], 1), (1, 2, i["norm_mix_post"][1], 0),
             (1, 4, i["norm_ffn_pre"][1], 1), (1, 3, None, 0), (1, 5, i["norm_ffn_post"][1], 0)]
    rest = np.concatenate([part(ada_w, l, n) for l, n, _, _ in order], axis=1)
    first = np.concatenate([part(ada_w, 0, 0), part(ada_w, 0, 1)], axis=1)
    one = np.ones(D, np.float32)
    vec = np.zeros((P, V_N), np.float32)

    def put(at, v):
        v = chunked(v)
        vec[:, at:at + v.shape[1]] = v

    put(V_NPRE, i["norm_mix_pre"][0])
    put(V_BSH, part(ada_b, 0, 0))
    put(V_BSC, part(ada_b, 0, 1))
    put(V_ADAB, np.concatenate([part(ada_b, l, n) for l, n, _, _ in order]))
    put(V_ONE, np.concatenate([one * o for _, _, _, o in order]))
    put(V_MUL, np.concatenate([one if m is None else m for _, _, m, _ in order]))
    cw = np.concatenate([i["ssm_conv_w"][0], i["ssm_conv_b"][0][None]], axis=0).reshape(TAPS + 1, 32, P)
    chunk = [[2 * g, 2 * g + 1, 2 * G + g, 3 * G + g] for g in range(G)]
    vec[:, V_CONV:V_SN] = cw[:, chunk, :].transpose(3, 1, 2, 0).reshape(P, -1)
    put(V_SN, i["ssm_norm"][0])
    put(V_CBI, i["cv_b_in"][0])
    vec[:, V_DW:V_DWB] = i["cv_dw_w"][0].reshape(TAP31, KD, P).transpose(2, 1, 0).reshape(P, -1)
    put(V_DWB, i["cv_dw_b"][0])
    put(V_LNG, i["cv_ln_g"][0])
    put(V_LNB, i["cv_ln_b"][0])
    w = i["ssm_w_in"][0]
    z0, x0, b0, c0, d0 = 0, 2 * D, 4 * D, 4 * D + G * P, 4 * D + 2 * G * P
    w_in = np.stack([k_major(np.concatenate([w[:, x0 + GW * g:x0 + GW * (g + 1)], w[:, b0 + P * g:b0 + P * (g + 1)],
                                             w[:, c0 + P * g:c0 + P * (g + 1)], w[:, z0 + GW * g:z0 + GW * (g + 1)]], axis=1)) for g in range(G)])
    gate_up = np.concatenate([i["exp_w_gate"].reshape(2, E, KD, P, F), i["exp_w_up"].reshape(2, E, KD, P, F)], axis=-1)
    return {
        "x": i["x"].reshape(TT, P, D),
        "ctx": i["ctx"].reshape(TT, P, D),
        "cvec": np.stack([chunked(i["c"][0]), chunked(i["c_ctx"])], axis=2),
        "consts": constants(),
        "vecs": vec,
        "rows": np.concatenate([i["ssm_d"][0], i["router_b"].reshape(-1), i["cv_b_out"][0]]),
        "dtcols": np.stack([i["ssm_dt_bias"][0].reshape(-1), i["ssm_a_log"][0].reshape(-1)], axis=1),
        "ada_first": np.stack([k_major(first[:, 512 * n:512 * (n + 1)]) for n in range(4)]),
        "ada_rest": rest.reshape(KD, P, G, ADA_G).transpose(2, 0, 1, 3).reshape(G * KD, P, ADA_G),
        "w_in": w_in,
        "w_dt": k_major(w[:, d0:]).reshape(P, KD, 64),
        "w_out": i["ssm_w_out"][0].reshape(G, 2, P, D).transpose(0, 2, 1, 3).reshape(G, P, 2 * D),
        "router_w": np.stack([k_major(i["router_w"][l]) for l in range(2)]),
        "gate_up": gate_up.transpose(0, 1, 3, 2, 4).reshape(2 * E, P, KD * 2 * F),
        "down": i["exp_w_down"].reshape(2 * E, 2, P, D).transpose(0, 2, 1, 3).reshape(2 * E, P, 2 * D),
        "sh_gate_up": np.stack([k_major(np.concatenate([i["sh_w_gate"][l], i["sh_w_up"][l]], axis=1)) for l in range(2)]),
        "sh_down": i["sh_w_down"].reshape(2, 2, P, D).transpose(0, 2, 1, 3).reshape(2, P, 2 * D),
        "cv_in": np.stack([k_major(np.concatenate([i["cv_w_in"][0][:, P * j:P * (j + 1)], i["cv_w_in"][0][:, D + P * j:D + P * (j + 1)]], axis=1)) for j in range(KD)]),
        "cv_out": k_major(i["cv_w_out"][0]),
    }


def program(nc, shapes):
    a = {}
    for name, (shape, dt) in shapes.items():
        a[name] = nc.dram_tensor("in_" + name, shape, dt, kind="ExternalInput").ap()
    a["out"] = nc.dram_tensor("out", (TT, P, D), F32, kind="ExternalOutput").ap()
    a["cs_scr"] = nc.dram_tensor("cs_scr", (64, T), F32).ap()
    a["ada_scr"] = nc.dram_tensor("ada_scr", (80, P), F32).ap()
    build(nc, a)


def kernel(**inputs):
    import concourse.bacc as bacc
    from concourse.bass_utils import run_bass_kernel_spmd

    arrays = {"in_" + n: np.ascontiguousarray(v) for n, v in layout({n: np.asarray(v) for n, v in inputs.items()}).items()}
    nc = bacc.Bacc("TRN2", target_bir_lowering=False, num_devices=1)
    program(nc, {n[3:]: (v.shape, mybir.dt.from_np(v.dtype)) for n, v in arrays.items()})
    r = run_bass_kernel_spmd(nc, [arrays], core_ids=[0])
    return r.results[0]["out"].reshape(1, T, D)
```

```python
from contextlib import ExitStack

import numpy as np
import concourse.bass as bass
from concourse import mybir

F32 = mybir.dt.float32
F32R = mybir.dt.float32r
BF16 = mybir.dt.bfloat16
I32 = mybir.dt.int32
ALU = mybir.AluOpType
ACT = mybir.ActivationFunctionType
AX = mybir.AxisListType
ds = bass.ds

P = 128
D = 1024
KD = D // P
T = 256
TT = T // P
G = 8
R = 4
PH = 64
GW = R * PH
TAPS = 5
WG = 2 * P + P + P + GW
EPS = 1e-6
E = 64
F = 256
CAP = 64
NOV = 36
NB = E + NOV
NPAIR = NB // 2
TAP31 = 31
ROW = 64
NROW = T // ROW
PADROW = ROW + TAP31 - 1
ADA_G = 10 * D // G
ADA_C = ADA_G // P
BIG = 1e30
GU_PAIR = 8192
DN_PAIR = 4096

C_ID, C_TU, C_TL, C_ONE, C_MF, C_MB = (P * i for i in range(6))
C_I64 = 6 * P
C_IOV = C_I64 + 64
C_LT8 = C_IOV + NOV
C_PIX = C_LT8 + 64
C_IE = C_PIX + 1
C_N = C_IE + E

V_NPRE = 0
V_BSH = V_NPRE + KD
V_BSC = V_BSH + KD
V_CONV = V_BSC + KD
V_SN = V_CONV + G * 4 * (TAPS + 1)
V_NPRE1 = V_SN + 2 * G
V_CBI = V_NPRE1 + KD
V_DW = V_CBI + 2 * KD
V_DWB = V_DW + KD * TAP31
V_LNG = V_DWB + KD
V_LNB = V_LNG + KD
V_N = V_LNB + KD

R_SD = 0
R_RB = 32
R_BO = R_RB + 2 * E
R_N = R_BO + D


class Chain:

    def __init__(self, eng, sem):
        self.eng, self.sem, self.base, self.n = eng, sem, 0, 0

    def at(self, base):
        self.base, self.n = base, 0

    def post(self, ins):
        ins.then_inc(self.sem, 1)
        self.n += 1

    def link(self, ins):
        self.post(ins)
        self.eng.wait_ge(self.sem, self.base + self.n)


def signal(eng, ins, sem, value):
    ins.then_inc(sem, 1)
    eng.wait_ge(sem, value)


class Core:

    def __init__(self, nc, ctx):
        self.nc, self.ctx, self.stage_sems = nc, ctx, []

    def sb(self, name, shape, dt=F32, ctx=None):
        return (ctx or self.ctx).enter_context(self.nc.sbuf_tensor(name, shape, dt))

    def ps(self, name, shape, dt=F32):
        return self.ctx.enter_context(self.nc.psum_tensor(name, shape, dt))

    def sem(self, name):
        self.stage_sems.append(self.nc.alloc_semaphore(name=name))
        return self.stage_sems[-1]

    def release(self):
        self.nc.clear_and_free_semaphores(self.stage_sems)
        self.nc.all_engine_barrier()
        self.stage_sems = []


def build(nc, a):
    with ExitStack() as ctx:
        c = Core(nc, ctx)
        c.gu = c.sb("gu", [P, 2 * GU_PAIR])
        c.dn = c.sb("dn", [P, 2 * DN_PAIR])
        c.x = c.sb("x", [P, TT, D])
        c.hT = c.sb("hT", [P, KD, 2 * T])
        c.cst = c.sb("cst", [P, C_N])
        c.vec = c.sb("vec", [P, V_N])
        c.rows = c.sb("rows", [P, R_N])
        c.adac = c.sb("adac", [P, 10 * G])
        c.pt = c.ps("pt", [P, 4, 512])
        c.pa = c.ps("pa", [P, 4, 512])
        c.const_landed = ctx.enter_context(nc.semaphore("const_landed"))
        with ExitStack() as s:
            b = ssm_buffers(c, s)
            modulate(nc, c, a, b)
            ssd(nc, c, a, b)
            c.release()
        for layer in range(2):
            with ExitStack() as s:
                m = moe_buffers(c, s, layer)
                if layer == 0:
                    ada_rows(nc, c, a, m)
                router(nc, c, a, m, layer)
                experts(nc, c, a, m, layer)
                ffn_end(nc, c, a, m, layer)
            if layer == 0:
                c.release()
                with ExitStack() as s:
                    conformer(nc, c, a, s)
                    c.release()



class Bag:
    pass


def ssm_buffers(c, s):
    b = Bag()
    sb = lambda name, shape, dt=F32: c.sb(name, shape, dt, s)
    b.cin = sb("conv_in", [P, 4, 2, T + TAPS - 1])
    b.cout = sb("conv_out", [P, 4, 2 * T])
    b.xs = sb("xs", [P, 4, GW])
    b.bt = sb("bt", [P, 4, P])
    b.cb = sb("cb", [P, 2, P])
    b.zs = sb("zs", [P, TT, GW])
    b.dec = sb("decay", [P, 2, R, 2, P])
    b.xu = sb("xu", [P, 6, GW])
    b.hs = sb("hs", [P, 4, GW])
    b.htmp = sb("htmp", [P, GW])
    b.y = sb("y", [P, TT, GW])
    b.ytmp = sb("ytmp", [P, TT, GW])
    b.yT = sb("yT", [P, 2, T])
    b.dt = sb("dtT", [P, 2, 4, 32])
    b.cs = sb("cs", [P, 2, 4, 32])
    b.ecs = sb("ecs", [P, 2, 4, 32])
    b.tot = sb("tot", [P, 2, 4, 32])
    b.uw = sb("uw", [P, 2, 4, 32])
    b.da = sb("daT", [P, 4, 64])
    b.csT = sb("csT", [64, T])
    b.col = sb("dtcol", [64, 4])
    b.adaacc = sb("adaacc", [P, ADA_G])
    b.adarow = sb("adarow", [1, ADA_G])
    b.cv = sb("cv", [P, KD, 2])
    b.scv = sb("scv", [P, KD, 2])
    b.mix = sb("mixcols", [P, 2, KD, 2])
    b.nrm = sb("nrm", [P, 8])
    return b


def sum_taps(dve, ch, c, b, g, part):
    dve.wait_ge(b.conv_in, 4 * g + part + 1)
    s0 = 0 if part < 3 else 1
    w = lambda tap: c.vec[:, ds(V_CONV + (4 * g + part) * (TAPS + 1) + tap, 1)]
    out = b.cout[:, part, :].rearrange("p (s l) -> p s l", s=2)[:, s0:2, :]
    at = lambda tap: b.cin[:, part, s0:2, tap:tap + T]
    ch.link(dve.tensor_scalar(out, at(0), w(0), w(TAPS), ALU.mult, ALU.add))
    for tap in range(1, TAPS):
        ins = dve.scalar_tensor_tensor(out=out, in0=at(tap), scalar=w(tap), in1=out, op0=ALU.mult, op1=ALU.add)
        if tap < TAPS - 1:
            ch.link(ins)
        else:
            signal(dve, ins, b.conv_sum, 4 * g + part + 1)


def modulate(nc, c, a, b):
    pt = c.pt
    w_landed = [c.sem(f"ada_landed{i}") for i in range(4)]
    cv_landed, x_landed, dtw_landed, stored = (c.sem(n) for n in ("cv_landed", "x_landed", "dtw_landed", "stored"))
    cv_ready, row_ps, row_sb, col_ps, mix_ready = (c.sem(n) for n in ("cv_ready", "row_ps", "row_sb", "col_ps", "mix_ready"))
    sumsq, rms_in, rms_sq, xn_ready, xt_ps, ht_act, ht_dve = (c.sem(n) for n in ("sumsq", "rms_in", "rms_sq", "xn_ready", "xt_ps", "ht_act", "ht_dve"))
    dt_ps, dt_z, dt_e, dt_u, dt_ln, dt_done, dtT_ps, dtT_sb, cs_ps, cs_sb, csT_sb, e_ready = (
        c.sem(n) for n in ("dt_ps", "dt_z", "dt_e", "dt_u", "dt_ln", "dt_done", "dtT_ps", "dtT_sb", "cs_ps", "cs_sb", "csT_sb", "e_ready"))
    mod_dve, mod_act = c.sem("mod_dve"), c.sem("mod_act")
    b.stored = stored
    b.win_landed = [c.sem(f"win_landed{i}") for i in range(2)]
    b.wout_landed = [c.sem(f"wout_landed{i}") for i in range(2)]
    b.csb_landed = c.sem("csb_landed")
    b.conv_in = c.sem("conv_in_ready")
    b.conv_sum = c.sem("conv_sum")
    b.proj_ps = c.sem("proj_ps")

    xn = c.dn[:, 0:4 * D].rearrange("p (q d) -> p q d", q=4)
    xc = b.dec[:].rearrange("p a r q l -> p (a r q l)")
    xq = [xc[:, 0:D], xc[:, D:2 * D], c.x[:, 0, :], c.x[:, 1, :]]
    wdt = c.dn[:, 4 * D:4 * D + KD * 64].rearrange("p (k n) -> p k n", k=KD)
    rows = b.cout[0:2].rearrange("p a b -> p (a b)")
    tmp = [c.gu[0:64, 6144 + 512 * i:6144 + 512 * (i + 1)] for i in range(4)]
    more = [c.gu[0:64, 14336 + 512 * i:14336 + 512 * (i + 1)] for i in range(3)]
    z, m, e, u = tmp
    d, ln, dtD = more
    ident = c.cst[:, C_ID:C_ID + P]
    win0 = c.gu[:, 0:KD * WG].rearrange("p (k n) -> p k n", k=KD)

    with nc.Block() as block:
        @block.sync
        def _(sp):
            def ada_tile(n):
                sp.dma_start(c.gu[:, 4096 * n:4096 * (n + 1)], a["ada_first"][n]).then_inc(w_landed[n], 16)

            sp.dma_start(b.cv[:], a["cvec"]).then_inc(cv_landed, 16)
            ada_tile(0)
            ada_tile(1)
            for t in range(2):
                sp.dma_start(xq[t], a["ctx"][t]).then_inc(x_landed, 16)
                sp.dma_start(xq[2 + t], a["x"][t]).then_inc(x_landed, 16)
            ada_tile(2)
            sp.dma_start(c.cst[:], a["consts"]).then_inc(c.const_landed, 16)
            sp.dma_start(c.vec[:], a["vecs"]).then_inc(c.const_landed, 16)
            sp.dma_start(c.rows[:], a["rows"].partition_broadcast(P)).then_inc(c.const_landed, 16)
            sp.dma_start(b.col[:, 0:2], a["dtcols"]).then_inc(c.const_landed, 16)
            ada_tile(3)
            sp.dma_start(wdt, a["w_dt"]).then_inc(dtw_landed, 16)
            sp.wait_ge(row_ps, 2)
            sp.dma_start(c.gu[:, 0:KD * WG], a["w_in"][0]).then_inc(b.win_landed[0], 16)
            sp.wait_ge(row_ps, 4)
            sp.dma_start(c.gu[:, GU_PAIR:GU_PAIR + KD * WG], a["w_in"][1]).then_inc(b.win_landed[1], 16)
            sp.wait_ge(xt_ps, 8)
            sp.dma_start(c.dn[:, 0:2 * D], a["w_out"][0]).then_inc(b.wout_landed[0], 16)
            sp.wait_ge(csT_sb, 1)
            sp.dma_start(a["cs_scr"], b.csT[:]).then_inc(stored, 16)
            sp.wait_ge(stored, 16)
            for dr in range(2):
                sp.dma_start(b.dec[:, dr].rearrange("p r q l -> p (r q l)"),
                             a["cs_scr"][32 * dr:32 * dr + R].rearrange("r l -> (r l)").partition_broadcast(P)).then_inc(b.csb_landed, 16)

        @block.tensor
        def _(pe):
            pe.wait_ge(cv_ready, 1)
            for n in range(4):
                pe.wait_ge(w_landed[n], 16)
                w = c.gu[:, 4096 * n:4096 * (n + 1)].rearrange("p (k n) -> p k n", k=KD)
                for k in range(KD):
                    mm = pe.matmul(pt[0:2, n, :], b.scv[:, k, :], w[:, k, :], start=k == 0, stop=k == KD - 1)
                mm.then_inc(row_ps, 1)
            pe.wait_ge(c.const_landed, 64)
            pe.wait_ge(row_sb, 4)
            for j in range(16):
                mm = pe.transpose(pt[:, 0, 2 * j:2 * j + 2], rows[:, P * j:P * (j + 1)], ident[0:2, 0:2])
            mm.then_inc(col_ps, 1)
            for q in range(4):
                pe.wait_ge(xn_ready, q + 1)
                for h in range(2):
                    if q == 0:
                        pe.wait_ge(mix_ready, 1)
                    if q >= 1:
                        pe.wait_ge(ht_act, 2 * (q - 1) + h + 1)
                        pe.wait_ge(ht_dve, 2 * (q - 1) + h + 1)
                    for k in range(4 * h, 4 * h + 4):
                        mm = pe.transpose(pt[:, 2 * h + k % 2, P * (k // 2 % 2):P * (k // 2 % 2 + 1)], xn[:, q, P * k:P * (k + 1)], ident)
                    mm.then_inc(xt_ps, 1)
            pe.wait_ge(dtw_landed, 16)
            pe.wait_ge(ht_act, 8)
            pe.wait_ge(ht_dve, 8)
            for k in range(KD):
                mm = pe.matmul(pt[0:64, 0, :], wdt[:, k, :], c.hT[:, k, :], start=k == 0, stop=k == KD - 1)
            mm.then_inc(dt_ps, 1)
            def first_proj(part):
                t0 = 0 if part < 3 else T
                for k in range(KD):
                    mm = pe.matmul(c.pa[:, part, 0:2 * T - t0], win0[:, k, P * part:P * (part + 1)], c.hT[:, k, t0:2 * T], start=k == 0, stop=k == KD - 1)
                mm.then_inc(b.proj_ps, 1)

            pe.wait_ge(b.win_landed[0], 16)
            first_proj(0)
            first_proj(1)
            pe.wait_ge(dt_done, 2)
            for i, src in enumerate((dtD, z)):
                for q in range(4):
                    mm = pe.transpose(pt[:, 1, 256 * i + 64 * q:256 * i + 64 * (q + 1)], src[:, P * q:P * (q + 1)], ident[0:64, 0:64])
            mm.then_inc(dtT_ps, 1)
            pe.wait_ge(dtT_sb, 1)
            tri = [c.cst[:, C_TU:C_TU + P], c.cst[:, C_TL:C_TL + P]]
            for dr in range(2):
                pe.matmul(pt[:, 2, P * dr:P * (dr + 1)], tri[dr], b.da[:, :, 32 * dr:32 * (dr + 1)], start=True, stop=True)
            pe.matmul(pt[:, 2, 256:512], c.cst[:, C_ONE:C_ONE + P], b.da[:].rearrange("p q n -> p (q n)"), start=True, stop=True).then_inc(cs_ps, 1)
            for dr in range(2):
                for q in range(2):
                    mm = pe.matmul(pt[32 * dr:32 * (dr + 1), 3, P * q:P * (q + 1)], b.da[:, 2 + q, 32 * dr:32 * (dr + 1)], tri[dr], start=True, stop=True)
            mm.then_inc(cs_ps, 1)
            first_proj(2)
            first_proj(3)

        @block.scalar
        def _(act):
            ch = Chain(act, mod_act)
            act.wait_ge(cv_landed, 16)
            signal(act, act.activation(b.scv[:].rearrange("p k n -> p (k n)"), b.cv[:].rearrange("p k n -> p (k n)"), ACT.Silu), cv_ready, 1)
            act.wait_ge(x_landed, 64)
            for q in range(4):
                signal(act, act.activation(b.cin[:].rearrange("p a b c -> p (a b c)")[:, 0:D], xq[q], ACT.Square, accum_out=b.nrm[:, q:q + 1]), sumsq, q + 1)
            act.wait_ge(rms_in, 1)
            signal(act, act.activation(b.nrm[:, 4:8], b.nrm[:, 0:4], ACT.Sqrt), rms_sq, 1)
            for n in range(4):
                act.wait_ge(row_ps, n + 1)
                signal(act, act.copy(rows[:, 512 * n:512 * (n + 1)], pt[0:2, n, :]), row_sb, n + 1)
            act.wait_ge(mix_ready, 1)
            for q in range(4):
                s = 1 if q < 2 else 0
                for h in range(2):
                    act.wait_ge(xt_ps, 2 * q + h + 1)
                    for k in (4 * h, 4 * h + 2):
                        ins = act.activation(c.hT[:, k, P * q:P * (q + 1)], pt[:, 2 * h, P * (k // 2 % 2):P * (k // 2 % 2 + 1)], ACT.Identity,
                                             bias=b.mix[:, 0, k, s:s + 1], scale=b.mix[:, 1, k, s:s + 1])
                        if k == 4 * h:
                            ch.post(ins)
                    signal(act, ins, ht_act, 2 * q + h + 1)
            act.wait_ge(c.const_landed, 64)
            ch.link(act.activation(b.col[:, 2:3], b.col[:, 1:2], ACT.Exp))
            act.wait_ge(dt_z, 1)
            ch.link(act.activation(e, z, ACT.Abs))
            signal(act, act.activation(e, e, ACT.Exp, scale=-1.0), dt_e, 1)
            act.wait_ge(dt_u, 1)
            signal(act, act.activation(ln, u, ACT.Ln), dt_ln, 1)
            for part in range(2):
                act.wait_ge(b.proj_ps, part + 1)
                signal(act, act.copy(b.cin[:, part, :, 2:2 + T], c.pa[:, part, :].rearrange("p (s l) -> p s l", s=2)), b.conv_in, part + 1)
            act.wait_ge(cs_sb, 1)
            cols = lambda t: t[:].rearrange("p a q n -> p (a q n)")
            ch.post(act.activation(cols(b.ecs), cols(b.cs), ACT.Exp))
            ch.post(act.activation(cols(b.uw), cols(b.uw), ACT.Exp))
            signal(act, act.activation(cols(b.tot), cols(b.tot), ACT.Exp), e_ready, 1)

        @block.vector
        def _(dve):
            ch = Chain(dve, mod_dve)
            dve.wait_ge(sumsq, 4)
            ch.post(dve.memset(b.adaacc[:], 0.0))
            ch.post(dve.memset(b.xu[:, 0, :], 0.0))
            ch.link(dve.memset(b.cin[:], 0.0))
            signal(dve, dve.tensor_scalar(b.nrm[:, 0:4], b.nrm[:, 0:4], 1.0 / D, EPS, ALU.mult, ALU.add), rms_in, 1)
            dve.wait_ge(rms_sq, 1)
            ch.link(dve.reciprocal(b.nrm[:, 4:8], b.nrm[:, 4:8]))
            for q in range(4):
                signal(dve, dve.tensor_scalar(xn[:, q, :], xq[q], b.nrm[:, 4 + q:5 + q], None, ALU.mult), xn_ready, q + 1)
            dve.wait_ge(c.const_landed, 64)
            dve.wait_ge(col_ps, 1)
            v = lambda o, n: c.vec[:, o:o + n].unsqueeze(2).broadcast_to([P, n, 2])
            cols = pt[:, 0, 0:32].rearrange("p (j n) -> p j n", n=2)
            ch.post(dve.tensor_tensor(b.mix[:, 0], cols[:, 0:KD], v(V_BSH, KD), ALU.add))
            ch.link(dve.tensor_tensor(b.mix[:, 1], cols[:, KD:2 * KD], v(V_BSC, KD), ALU.add))
            signal(dve, dve.scalar_tensor_tensor(out=b.mix[:, 1], in0=b.mix[:, 1], scalar=1.0, in1=v(V_NPRE, KD), op0=ALU.add, op1=ALU.mult), mix_ready, 1)
            for q in range(4):
                s = 1 if q < 2 else 0
                for h in range(2):
                    dve.wait_ge(xt_ps, 2 * q + h + 1)
                    for k in (4 * h + 1, 4 * h + 3):
                        ins = dve.tensor_scalar(c.hT[:, k, P * q:P * (q + 1)], pt[:, 2 * h + 1, P * (k // 2 % 2):P * (k // 2 % 2 + 1)],
                                                b.mix[:, 1, k, s:s + 1], b.mix[:, 0, k, s:s + 1], ALU.mult, ALU.add)
                        if k == 4 * h + 1:
                            ch.post(ins)
                    signal(dve, ins, ht_dve, 2 * q + h + 1)
            dve.wait_ge(dt_ps, 1)
            dve.wait_ge(row_ps, 4)
            signal(dve, dve.tensor_scalar(z, pt[0:64, 0, :], b.col[:, 0:1], None, ALU.add), dt_z, 1)
            ch.link(dve.tensor_scalar(m, z, 0.0, None, ALU.max))
            dve.wait_ge(dt_e, 1)
            signal(dve, dve.tensor_scalar(u, e, 1.0, None, ALU.add), dt_u, 1)
            ch.link(dve.tensor_scalar(d, u, 1.0, None, ALU.subtract))
            ch.link(dve.tensor_tensor(d, e, d, ALU.subtract))
            dve.wait_ge(dt_ln, 1)
            ch.link(dve.reciprocal(u, u))
            ch.link(dve.tensor_tensor(d, d, u, ALU.mult))
            ch.link(dve.tensor_tensor(m, m, ln, ALU.add))
            signal(dve, dve.tensor_tensor(dtD, m, d, ALU.add), dt_done, 1)
            signal(dve, dve.tensor_scalar(z, dtD, b.col[:, 2:3], -1.0, ALU.mult, ALU.mult), dt_done, 2)
            sum_taps(dve, ch, c, b, 0, 0)
            dve.wait_ge(dtT_ps, 1)
            for dr in range(2):
                ch.post(dve.tensor_copy(b.dt[:, dr], pt[:, 1, 0:256].rearrange("p (q a n) -> p a q n", q=4, a=2)[:, dr]))
            ins = dve.tensor_copy(b.da[:].rearrange("p q n -> p (q n)"), pt[:, 1, 256:512])
            signal(dve, ins, dtT_sb, 1)
            dve.wait_ge(cs_ps, 1)
            for dr in range(2):
                ch.post(dve.tensor_copy(b.cs[:, dr].rearrange("p q n -> p (q n)"), pt[:, 2, P * dr:P * (dr + 1)]))
            for dr in range(2):
                ch.link(dve.tensor_copy(b.tot[:, dr], pt[:, 2, 256:512].rearrange("p (q a n) -> p a q n", q=4, a=2)[:, dr]))
            signal(dve, dve.tensor_tensor(b.uw[:].rearrange("p a q n -> p (a q n)"), b.tot[:].rearrange("p a q n -> p (a q n)"),
                                          b.cs[:].rearrange("p a q n -> p (a q n)"), ALU.subtract), cs_sb, 1)
            dve.wait_ge(cs_ps, 2)
            signal(dve, dve.tensor_copy(b.csT[:], pt[0:64, 3, 0:256]), csT_sb, 1)
            dve.wait_ge(e_ready, 1)
            ch.link(dve.tensor_tensor(b.uw[:].rearrange("p a q n -> p (a q n)"), b.uw[:].rearrange("p a q n -> p (a q n)"),
                                      b.dt[:].rearrange("p a q n -> p (a q n)"), ALU.mult))
            sum_taps(dve, ch, c, b, 0, 1)



def ssd(nc, c, a, b):
    pt, pa = c.pt, c.pa
    XC, BC, CC = 0, 2, 3
    proj_ps = b.proj_ps
    conv_in, conv_sum = b.conv_in, b.conv_sum
    conv_act = c.sem("conv_act")
    z_ready, ada_col, ada_used = (c.sem(n) for n in ("z_ready", "ada_col", "ada_used"))
    ada_sb, ada_scaled = c.sem("ada_sb"), c.sem("ada_scaled")
    tr_ps, tr_sb = c.sem("tr_ps"), c.sem("tr_sb")
    xu_ready, st_ps, st_ready = c.sem("xu_ready"), c.sem("st_ps"), c.sem("st_ready")
    diff_ready, exp_ready, m_ready = c.sem("diff_ready"), c.sem("exp_ready"), c.sem("m_ready")
    y_ps, y_sum, y_gated, ysq, yms, yrt, yn_ready = (c.sem(n) for n in ("y_ps", "y_sum", "y_gated", "ysq", "yms", "yrt", "yn_ready"))
    yT_ps, yT_sb, out_ps = c.sem("yT_ps"), c.sem("yT_sb"), c.sem("out_ps")
    ada_landed = [c.sem(f"ada_tile{i}") for i in range(4)]
    ssd_dve, ssd_act = c.sem("ssd_dve"), c.sem("ssd_act")
    ident = c.cst[:, C_ID:C_ID + P]
    ada_tile = [c.dn[:, 4096:4096 + ADA_G], c.dn[:, 4096 + ADA_G:4096 + 2 * ADA_G],
                c.gu[:, 6144:6144 + ADA_G], c.gu[:, 14336:14336 + ADA_G]]
    win = [c.gu[:, GU_PAIR * s:GU_PAIR * s + KD * WG].rearrange("p (k n) -> p k n", k=KD) for s in range(2)]
    wout = [c.dn[:, 2 * D * s:2 * D * (s + 1)].rearrange("p (j n) -> p j n", j=2) for s in range(2)]
    heads = lambda t, dr, q0, q1, g: t[:, dr, q0:q1, ds(R * g, R)]
    wide = lambda ap, q: ap.unsqueeze(3).broadcast_to([P, q, R, PH])
    as_heads = lambda ap: ap.rearrange("p q (r n) -> p q r n", r=R)

    def over_groups(eng, body):
        with eng.Fori(0, G // 2 - 1) as i:
            body(2 * i, 0, True, True)
            body(2 * i + 1, 1, True, True)
        body(G - 2, 0, True, False)
        body(G - 1, 1, False, False)

    with nc.Block() as block:
        @block.sync
        def _(sp):
            def group(g, slot, following, two_following):
                if two_following:
                    sp.wait_ge(proj_ps, 5 * g + 5)
                    sp.dma_start(c.gu[:, GU_PAIR * slot:GU_PAIR * slot + KD * WG],
                                 a["w_in"][ds(g + 2, 1)].rearrange("g p n -> (g p) n")).then_inc(b.win_landed[slot], 16)
                if following:
                    sp.wait_ge(y_ps, g + 1)
                    sp.dma_start(c.dn[:, 2 * D * (1 - slot):2 * D * (2 - slot)],
                                 a["w_out"][ds(g + 1, 1)].rearrange("g p n -> (g p) n")).then_inc(b.wout_landed[1 - slot], 16)
                    for dr in range(2):
                        sp.dma_start(b.dec[:, dr].rearrange("p r q l -> p (r q l)"),
                                     a["cs_scr"][ds(32 * dr + R * (g + 1), R)].rearrange("r l -> (r l)").partition_broadcast(P)).then_inc(b.csb_landed, 16)
                sp.wait_ge(ada_sb, g + 1)
                sp.dma_start(a["ada_raw"][ds(g, 1)], b.adarow[:]).then_inc(b.stored, 16)
            over_groups(sp, group)
            sp.wait_ge(b.stored, 16 * G + 16)

        @block.gpsimd
        def _(pool):
            def load(tile, k):
                pool.dma_start(ada_tile[k % 4], a["ada_rest"][ds(tile, 1)].rearrange("g p n -> (g p) n")).then_inc(ada_landed[k % 4], 16)

            def group(g, last):
                for k in range(KD):
                    if k >= 2:
                        pool.wait_ge(ada_used, (KD - 1) * g + k - 1)
                    elif k == 0 and (not isinstance(g, int) or g > 0):
                        pool.wait_ge(ada_used, (KD - 1) * g)
                    if k >= 1:
                        pool.wait_ge(ada_scaled, KD * g + k + 1)
                    if not last or k + 3 < KD:
                        load(KD * g + k + 3, k + 3)
                    if k >= 1:
                        pool.tensor_tensor(b.adaacc[:], b.adaacc[:], ada_tile[k % 4], ALU.add).then_inc(ada_used, 1)

            for k in range(3):
                load(k, k)
            group(0, False)
            with pool.Fori(1, G - 1) as g:
                group(g, False)
            group(G - 1, True)

        @block.tensor
        def _(pe):
            def proj(g, slot, part, tiles=range(TT)):
                w = win[slot]
                if part == 0:
                    pe.wait_ge(b.win_landed[slot], 16 * (g // 2) + 16 if isinstance(g, int) else 8 * (g - slot) + 16)
                if part < 3:
                    for k in range(KD):
                        mm = pe.matmul(pt[:, 0, :], w[:, k, P * part:P * (part + 1)], c.hT[:, k, :], start=k == 0, stop=k == KD - 1)
                elif part == 3:
                    for k in range(KD):
                        mm = pe.matmul(pt[:, 1, 0:T], w[:, k, 3 * P:4 * P], c.hT[:, k, T:2 * T], start=k == 0, stop=k == KD - 1)
                else:
                    for t in tiles:
                        for k in range(KD):
                            mm = pe.matmul(pt[:, 3, GW * t:GW * (t + 1)], c.hT[:, k, T + P * t:T + P * (t + 1)], w[:, k, 4 * P:4 * P + GW],
                                           start=k == 0, stop=k == KD - 1)
                if part < 4 or TT - 1 in tiles:
                    mm.then_inc(proj_ps, 1)

            def ada(g):
                pe.wait_ge(ada_used, (KD - 1) * g + KD - 1)
                for n in range(3):
                    cols = slice(512 * n, min(512 * (n + 1), ADA_G))
                    mm = pe.matmul(pt[0:1, 1 + n, 0:cols.stop - cols.start], c.cst[:, C_ONE:C_ONE + 1], b.adaacc[:, cols], start=True, stop=True)
                mm.then_inc(ada_col, 1)

            def group(g, slot, following, two_following):
                pe.wait_ge(conv_act, 4 * g + 4)
                for ch2 in range(2):
                    for q in range(4):
                        mm = pe.transpose(pt[:, q // 2, GW * (q % 2) + P * ch2:GW * (q % 2) + P * (ch2 + 1)], b.cout[:, XC + ch2, P * q:P * (q + 1)], ident)
                mm.then_inc(tr_ps, 1)
                for q in range(4):
                    mm = pe.transpose(pt[:, 2, P * q:P * (q + 1)], b.cout[:, BC, P * q:P * (q + 1)], ident)
                mm.then_inc(tr_ps, 1)
                pe.wait_ge(z_ready, g + 1)
                for q in range(2):
                    mm = pe.matmul(pt[:, 3, P * q:P * (q + 1)], b.cout[:, BC, T + P * q:T + P * (q + 1)], b.cout[:, CC, T + P * q:T + P * (q + 1)], start=True, stop=True)
                mm.then_inc(tr_ps, 1)
                if following:
                    pe.wait_ge(tr_sb, 4 * g + 1)
                    proj(g + 1, 1 - slot, 0)
                pe.wait_ge(tr_sb, 4 * g + 4)
                pe.wait_ge(xu_ready, g + 1)
                for n, q in enumerate((0, 1, 2, 1, 0, 3)):
                    u = (0, 1, 2, 4, 3, 5)[n]
                    mm = pe.matmul(pt[:, 1 + n // 2, GW * (n % 2):GW * (n % 2 + 1)], b.bt[:, q, :], b.xu[:, u, :], start=True, stop=True)
                mm.then_inc(st_ps, 1)
                if following:
                    pe.wait_ge(conv_in, 4 * g + 5)
                    proj(g + 1, 1 - slot, 1)
                pe.wait_ge(st_ready, g + 1)
                for h in range(R):
                    pe.wait_ge(m_ready, g + 1)
                    for q in range(2):
                        pe.matmul(pt[:, 1, GW * q + PH * h:GW * q + PH * (h + 1)], b.dec[:, 0, h, q, :], b.xs[:, 2 + q, PH * h:PH * (h + 1)], start=True, stop=True)
                for dr in range(2):
                    for q in range(2):
                        mm = pe.matmul(pt[:, 2 + dr, GW * q:GW * (q + 1)], b.cout[:, CC, T + P * q:T + P * (q + 1)],
                                       b.hs[:, 2 * dr + (q if dr == 0 else 1 - q), :], start=True, stop=True)
                mm.then_inc(y_ps, 1)
                if following:
                    pe.wait_ge(conv_in, 4 * g + 6)
                    proj(g + 1, 1 - slot, 2)
                    pe.wait_ge(y_sum, g + 1)
                    proj(g + 1, 1 - slot, 3)
                    proj(g + 1, 1 - slot, 4, tiles=(0,))
                pe.wait_ge(yn_ready, g + 1)
                for t in range(TT):
                    for j in range(2):
                        mm = pe.transpose(pt[:, 2, T * j + P * t:T * j + P * (t + 1)], b.y[:, t, P * j:P * (j + 1)], ident)
                mm.then_inc(yT_ps, 1)
                if following:
                    proj(g + 1, 1 - slot, 4, tiles=(1,))
                pe.wait_ge(yT_sb, g + 1)
                pe.wait_ge(b.wout_landed[slot], 16 * (g // 2) + 16 if isinstance(g, int) else 8 * (g - slot) + 16)
                for t in range(TT):
                    for h in range(2):
                        for j in range(2):
                            mm = pe.matmul(pa[:, 2 * t + h, :], b.yT[:, j, P * t:P * (t + 1)], wout[slot][:, j, 512 * h:512 * (h + 1)],
                                           start=False, stop=False, skip_group_check=True)
                    if t == 0:
                        if following:
                            pe.wait_ge(conv_in, 4 * g + 8)
                            pe.wait_ge(z_ready, g + 2)
                        ada(g)
                mm.then_inc(out_ps, 1)
                pe.wait_ge(ada_sb, g + 1)

            proj(0, 0, 4)
            zeros = b.xu[:, 0, :].bitcast(BF16)
            for n in range(4):
                pe.wait_ge(conv_in, n + 1)
                pe.matmul(pa[:, n, :], zeros[:, 0:P], zeros, start=True, stop=False, skip_group_check=True)
            over_groups(pe, group)

        @block.scalar
        def _(act):
            ch = Chain(act, ssd_act)

            def take(g, part):
                act.wait_ge(proj_ps, 5 * g + part + 1)
                if not isinstance(g, int) or g > 0:
                    act.wait_ge(conv_sum, 4 * g + part - 3)
                first = isinstance(g, int) and g == 0
                if part < 3:
                    ins = act.copy(b.cin[:, part, :, 2:2 + T], (pa[:, part, :] if first else pt[:, 0, :]).rearrange("p (s l) -> p s l", s=2))
                else:
                    ins = act.copy(b.cin[:, part, 1, 2:2 + T], pa[:, part, 0:T] if first else pt[:, 1, 0:T])
                signal(act, ins, conv_in, 4 * g + part + 1)

            def silu(g, part):
                act.wait_ge(conv_sum, 4 * g + part + 1)
                ap = b.cout[:, part, :] if part < 3 else b.cout[:, part, T:2 * T]
                signal(act, act.activation(ap, ap, ACT.Silu), conv_act, 4 * g + part + 1)

            def decays(g):
                act.wait_ge(diff_ready, g + 1)
                e = b.dec[:].rearrange("p d r q l -> p (d r q l)")
                signal(act, act.activation(e, e, ACT.Exp), exp_ready, g + 1)

            def scale_tiles(g, ks):
                for k in ks:
                    act.wait_ge(ada_landed[k % 4], 32 * g + 16 * (k // 4) + 16)
                    act.activation(ada_tile[k % 4] if k else b.adaacc[:], ada_tile[k % 4], ACT.Copy, scale=b.scv[:, k, 0:1]).then_inc(ada_scaled, 1)

            def take_z(g):
                act.wait_ge(proj_ps, 5 * g + 5)
                if not isinstance(g, int) or g > 0:
                    act.wait_ge(y_gated, g)
                signal(act, act.activation(b.zs[:].rearrange("p t n -> p (t n)"), pt[:, 3, :], ACT.Silu), z_ready, g + 1)

            def group(g, slot, following, two_following):
                ch.at(2 * g)
                act.wait_ge(tr_ps, 3 * g + 1)
                for n in range(2):
                    signal(act, act.copy(b.xs[:, 2 * n:2 * n + 2, :].rearrange("p q n -> p (q n)"), pt[:, n, :]), tr_sb, 4 * g + n + 1)
                act.wait_ge(tr_ps, 3 * g + 2)
                signal(act, act.copy(b.bt[:].rearrange("p q n -> p (q n)"), pt[:, 2, :]), tr_sb, 4 * g + 3)
                act.wait_ge(tr_ps, 3 * g + 3)
                signal(act, act.copy(b.cb[:].rearrange("p q n -> p (q n)"), pt[:, 3, 0:2 * P]), tr_sb, 4 * g + 4)
                decays(g)
                scale_tiles(g, (0, 1))
                if following:
                    take(g + 1, 0)
                scale_tiles(g, (2, 3))
                if following:
                    take(g + 1, 1)
                    silu(g + 1, 0)
                scale_tiles(g, (4, 5))
                if following:
                    take(g + 1, 2)
                scale_tiles(g, (6,))
                act.wait_ge(y_gated, g + 1)
                for t in range(TT):
                    ins = act.activation(b.ytmp[:, t, :], b.y[:, t, :], ACT.Square, accum_out=b.nrm[:, t:t + 1])
                    if t == 0:
                        ch.link(ins)
                signal(act, ins, ysq, g + 1)
                act.wait_ge(yms, g + 1)
                signal(act, act.activation(b.nrm[:, 2:4], b.nrm[:, 0:2], ACT.Sqrt), yrt, g + 1)
                if following:
                    silu(g + 1, 1)
                    take(g + 1, 3)
                scale_tiles(g, (7,))
                act.wait_ge(yT_ps, g + 1)
                for j in range(2):
                    ins = act.activation(b.yT[:, j, :], pt[:, 2, T * j:T * (j + 1)], ACT.Copy, scale=c.vec[:, ds(V_SN + 2 * g + j, 1)])
                    if j == 0:
                        ch.link(ins)
                signal(act, ins, yT_sb, g + 1)
                if following:
                    silu(g + 1, 2)
                    take_z(g + 1)
                    silu(g + 1, 3)
                act.wait_ge(b.stored, 16 * g + 16)
                act.wait_ge(ada_col, g + 1)
                signal(act, act.copy(b.adarow[:], pt[0:1, 1:4, :].rearrange("p b n -> p (b n)")[:, 0:ADA_G]), ada_sb, g + 1)
                assert ch.n == 2

            take(0, 2)
            take(0, 3)
            silu(0, 0)
            silu(0, 1)
            silu(0, 2)
            silu(0, 3)
            take_z(0)
            over_groups(act, group)

        @block.vector
        def _(dve):
            ch = Chain(dve, ssd_dve)
            START, STEPS = 11, 38

            def taps(g, part):
                if not isinstance(g, int) or g > 0:
                    dve.wait_ge(tr_ps if part < 3 else y_ps, 3 * g if part < 3 else g)
                sum_taps(dve, ch, c, b, g, part)

            def exponents(g):
                dve.wait_ge(b.csb_landed, 32 * g + 32)
                for dr in range(2):
                    e = b.dec[:, dr]
                    csq = b.cs[:, dr, 2:4, ds(R * g, R)].rearrange("p q r -> p r q").unsqueeze(3).broadcast_to([P, R, 2, P])
                    ch.link(dve.tensor_tensor(e, e, csq, ALU.subtract))
                    mask = c.cst[:, (C_MF, C_MB)[dr]:(C_MF, C_MB)[dr] + P].unsqueeze(1).broadcast_to([P, 2 * R, P])
                    e2 = e.rearrange("p r q l -> p (r q) l")
                    ins = dve.tensor_tensor(e2, e2, mask, ALU.min)
                    if dr == 0:
                        ch.link(ins)
                signal(dve, ins, diff_ready, g + 1)

            def weigh(g):
                dve.wait_ge(exp_ready, g + 1)
                for dr in range(2):
                    dtq = b.dt[:, dr, 2:4, ds(R * g, R)].rearrange("p q r -> p r q").unsqueeze(3).broadcast_to([P, R, 2, P])
                    ins = dve.tensor_tensor(b.dec[:, dr], b.dec[:, dr], dtq, ALU.mult)
                    ch.post(ins) if dr == 0 else ch.link(ins)
                ch.link(dve.tensor_tensor(b.dec[:, 0], b.dec[:, 0], b.dec[:, 1], ALU.add))

            def group(g, slot, following, two_following):
                ch.at(START + STEPS * g)
                dve.wait_ge(tr_sb, 4 * g + 2)
                for u0, q0, q1, dr in ((0, 0, 3, 0), (3, 0, 2, 1)):
                    ch.post(dve.tensor_tensor(as_heads(b.xu[:, u0:u0 + q1 - q0, :]), as_heads(b.xs[:, q0:q1, :]), wide(heads(b.uw, dr, q0, q1, g), q1 - q0), ALU.mult))
                signal(dve, dve.tensor_tensor(as_heads(b.xu[:, 5:6, :]), as_heads(b.xs[:, 3:4, :]), wide(heads(b.uw, 1, 3, 4, g), 1), ALU.mult), xu_ready, g + 1)
                weigh(g)
                dve.wait_ge(tr_sb, 4 * g + 4)
                m = b.dec[:, 0].rearrange("p r q l -> p r (q l)")
                signal(dve, dve.tensor_tensor(m, m, b.cb[:].rearrange("p q l -> p (q l)").unsqueeze(1).broadcast_to([P, R, 2 * P]), ALU.mult), m_ready, g + 1)
                dve.wait_ge(st_ps, g + 1)
                S = lambda n: pt[:, 1 + n // 2, GW * (n % 2):GW * (n % 2 + 1)]
                head = lambda ap: ap.rearrange("p (r n) -> p r n", r=R)
                for dr in range(2):
                    dq = ((1, 2), (0, 3))[dr]
                    dec = lambda q: b.tot[:, dr, q, ds(R * g, R)].unsqueeze(2).broadcast_to([P, R, PH])
                    h1, h2 = b.hs[:, 2 * dr, :], b.hs[:, 2 * dr + 1, :]
                    ch.link(dve.tensor_tensor(head(b.htmp[:]), head(S(3 * dr)), dec(dq[0]), ALU.mult))
                    ch.link(dve.tensor_tensor(h1, b.htmp[:], S(3 * dr + 1), ALU.add))
                    ch.link(dve.tensor_tensor(head(b.htmp[:]), head(h1), dec(dq[1]), ALU.mult))
                    ins = dve.tensor_tensor(h2, b.htmp[:], S(3 * dr + 2), ALU.add)
                    if dr == 0:
                        ch.link(ins)
                signal(dve, ins, st_ready, g + 1)
                if following:
                    taps(g + 1, 0)
                y, yt = b.y[:], b.ytmp[:]
                skip = c.rows[:, ds(R_SD + R * g, R)].unsqueeze(1).unsqueeze(3).broadcast_to([P, 2, R, PH])
                ch.link(dve.tensor_tensor(as_heads(y), as_heads(b.xs[:, 2:4, :]), skip, ALU.mult))
                dve.wait_ge(y_ps, g + 1)
                bank = lambda n: pt[:, n, :].rearrange("p (q n) -> p q n", q=2)
                ch.link(dve.tensor_tensor(as_heads(yt), as_heads(bank(2)), wide(heads(b.ecs, 0, 2, 4, g), 2), ALU.mult))
                ch.link(dve.tensor_tensor(y, y, yt, ALU.add))
                ch.link(dve.tensor_tensor(as_heads(yt), as_heads(bank(3)), wide(heads(b.ecs, 1, 2, 4, g), 2), ALU.mult))
                ch.link(dve.tensor_tensor(y, y, yt, ALU.add))
                signal(dve, dve.tensor_tensor(y, y, bank(1), ALU.add), y_sum, g + 1)
                dve.wait_ge(z_ready, g + 1)
                signal(dve, dve.tensor_tensor(y, y, b.zs[:], ALU.mult), y_gated, g + 1)
                if following:
                    taps(g + 1, 1)
                dve.wait_ge(ysq, g + 1)
                signal(dve, dve.tensor_scalar(b.nrm[:, 0:2], b.nrm[:, 0:2], 1.0 / GW, EPS, ALU.mult, ALU.add), yms, g + 1)
                dve.wait_ge(yrt, g + 1)
                ch.link(dve.reciprocal(b.nrm[:, 4:6], b.nrm[:, 2:4]))
                for t in range(TT):
                    ins = dve.tensor_scalar(b.y[:, t, :], b.y[:, t, :], b.nrm[:, 4 + t:5 + t], None, ALU.mult)
                    if t == 0:
                        ch.link(ins)
                signal(dve, ins, yn_ready, g + 1)
                if following:
                    taps(g + 1, 2)
                    taps(g + 1, 3)
                    exponents(g + 1)
                assert ch.n == STEPS or not following, ch.n

            exponents(0)
            taps(0, 2)
            taps(0, 3)
            assert ch.n == START, ch.n
            over_groups(dve, group)



def moe_buffers(c, s, layer):
    m = Bag()
    sb = lambda name, shape, dt=F32: c.sb(f"{name}{layer}", shape, dt, s)
    m.bc = sb("bc", [P, 3, D])
    m.hr = sb("hr", [P, 2, TT, D], F32R)
    m.work = sb("work", [P, 2048])
    m.ys = sb("ys", [P, 2, D], F32R)
    m.sr = sb("sr", [P, TT, P], F32R)
    m.sb = sb("sb", [P, TT, P], BF16)
    m.st = sb("st", [P, T], F32R)
    m.rk = sb("rk", [P, NPAIR, TT, 2])
    m.wb = sb("wb", [P, NPAIR, TT, 3, 2], BF16)
    m.act = sb("act", [P, F])
    m.sg = sb("sg", [P, 2 * F])
    m.actT = sb("actT", [P, 2, T])
    m.wsl = sb("wsl", [P, 1])
    m.nrm = sb("mnrm", [P, 16])
    m.rw = sb("rw", [P, KD, E])
    m.idb = sb("idb", [P, P], BF16)
    m.tub = sb("tub", [P, P], BF16)
    m.oneb = sb("oneb", [P, P], BF16)
    m.negb = sb("negb", [E, P], BF16)
    m.pixb = sb("pixb", [P, 1], BF16)
    m.rt = sb("rt", [P, 9, 2 * E])
    m.rb = sb("rbf", [P, 5, TT, E], BF16)
    m.trb = sb("trb", [E, 8, P], BF16)
    m.oh = sb("oh", [E, NB], BF16)
    m.jm = sb("jm", [E, NOV], BF16)
    m.nbb = sb("nbb", [E, 1], BF16)
    m.col = sb("mcol", [E, 8])
    m.ov = sb("ov", [E, 3, NOV])
    m.tab = sb("tab", [1, NB + 1], I32)
    m.gu_landed = [[[c.sem(f"gu_landed{layer}{s}{ab}{half}") for half in range(2)] for ab in range(2)] for s in range(2)]
    m.dn_landed = [[c.sem(f"dn_landed{layer}{s}{ab}") for ab in range(2)] for s in range(2)]
    m.bc_landed = c.sem(f"bc_landed{layer}")
    return m


def load_gate_up(sp, c, a, m, layer, slot, ab, expert, half):
    n = GU_PAIR // 4
    at = GU_PAIR * slot + GU_PAIR // 2 * ab + n * half
    sp.dma_start(c.gu[:, at:at + n], a["gate_up"][ds(E * layer + expert, 1), :, n * half:n * (half + 1)].rearrange("e p n -> (e p) n")).then_inc(m.gu_landed[slot][ab][half], 16)


def load_down(sp, c, a, m, layer, slot, ab, expert):
    at = DN_PAIR * slot + DN_PAIR // 2 * ab
    sp.dma_start(c.dn[:, at:at + DN_PAIR // 2], a["down"][ds(E * layer + expert, 1)].rearrange("e p n -> (e p) n")).then_inc(m.dn_landed[slot][ab], 16)


def ada_rows(nc, c, a, m):
    raw_landed, done, c.rows_out, turned, ada_dve = (c.sem(n) for n in ("raw_landed", "ada_done", "rows_out", "ada_turned", "ada_dve"))
    chunks = m.work[0:80, 0:P]
    bias, one, mul = (m.work[0:80, P * (n + 1):P * (n + 2)] for n in range(3))
    with nc.Block() as block:
        @block.sync
        def _(sp):
            sp.dma_start(chunks, a["ada_raw"].rearrange("g (k p) -> (g k) p", p=P)).then_inc(raw_landed, 16)
            sp.dma_start(m.work[0:80, P:4 * P], a["ada_par"]).then_inc(raw_landed, 16)
            sp.wait_ge(done, 1)
            sp.dma_start(a["ada_scr"], chunks).then_inc(c.rows_out, 16)
            sp.wait_ge(c.rows_out, 16)

        @block.vector
        def _(dve):
            ch = Chain(dve, ada_dve)
            dve.wait_ge(raw_landed, 32)
            ch.link(dve.tensor_tensor(chunks, chunks, bias, ALU.add))
            ch.link(dve.tensor_tensor(chunks, chunks, one, ALU.add))
            signal(dve, dve.tensor_tensor(chunks, chunks, mul, ALU.mult), done, 1)

        @block.tensor
        def _(pe):
            pe.wait_ge(done, 1)
            pe.transpose(c.pt[:, 0, 0:80], chunks, c.cst[0:80, C_ID:C_ID + 80]).then_inc(turned, 1)

        @block.scalar
        def _(act):
            act.wait_ge(turned, 1)
            act.copy(c.adac[:], c.pt[:, 0, 0:80])


def bc_row(a, r):
    return a["ada_scr"][KD * r:KD * (r + 1)].rearrange("k p -> (k p)").partition_broadcast(P)


def router(nc, c, a, m, layer):
    pt, pa = c.pt, c.pa
    L = str(layer)
    sem = lambda n: c.sem(n + L)
    w_landed, sgw_landed = sem("rw_landed"), sem("sgw_landed")
    y_sq, y_ms, y_rt, x_new, x_sq, x_ms, x_rt, h_ready, h_hi, h_lo = (
        sem(n) for n in ("y_sq", "y_ms", "y_rt", "x_new", "x_sq", "x_ms", "x_rt", "h_ready", "h_hi", "h_lo"))
    ht_ps, ht_sb, lg_ps, scores, sgu_ps, sgu_act, sact_ready, casts = (
        sem(n) for n in ("ht_ps", "ht_sb", "lg_ps", "scores", "sgu_ps", "sgu_act", "sact_ready", "casts"))
    chosen, cum_ps, parts, tr_ps, tr_sb, oh_ready, tab_ps, shared_done = (
        sem(n) for n in ("chosen", "cum_ps", "parts", "rtr_ps", "rtr_sb", "oh_ready", "tab_ps", "shared_done"))
    r_dve, r_act = sem("r_dve"), sem("r_act")
    ident = c.cst[:, C_ID:C_ID + P]
    hreg = [c.hT[:, 4 * t:4 * t + 4, T:2 * T] for t in range(TT)]
    as4 = lambda ap: ap.rearrange("p (k n) -> p k n", k=4)
    sgw = c.dn[:, DN_PAIR:2 * DN_PAIR].rearrange("p (k n) -> p k n", k=KD)
    sdw = m.work[:].rearrange("p (j n) -> p j n", j=2)
    row = (0, 6)[layer]
    sc, sel, m8, cmp, cmp2, msel, rep, sm, w = (m.rt[:, i, :] for i in range(9))
    per_t = lambda ap: ap.rearrange("p (t e) -> p t e", t=TT)
    y = lambda t: pa[:, 2 * t:2 * t + 2, :].rearrange("p b n -> p (b n)")

    with nc.Block() as block:
        @block.sync
        def _(sp):
            for n in range(3):
                sp.dma_start(m.bc[:, n, :], bc_row(a, row + n)).then_inc(m.bc_landed, 16)
            sp.dma_start(m.rw[:].rearrange("p k e -> p (k e)"), a["router_w"][layer]).then_inc(w_landed, 16)
            sp.dma_start(c.dn[:, DN_PAIR:2 * DN_PAIR], a["sh_gate_up"][layer]).then_inc(sgw_landed, 16)
            sp.dma_start(m.work[:], a["sh_down"][layer]).then_inc(sgw_landed, 16)
            for slot in range(2):
                for half in range(2):
                    for ab in range(2):
                        load_gate_up(sp, c, a, m, layer, slot, ab, 2 * slot + ab, half)
                if slot == 1:
                    sp.wait_ge(sgu_ps, 2)
                for ab in range(2):
                    load_down(sp, c, a, m, layer, slot, ab, 2 * slot + ab)

        @block.tensor
        def _(pe):
            for n in range(4):
                for k in (2 * n, 2 * n + 1):
                    for t in range(TT):
                        if n == 0:
                            pe.wait_ge(h_ready, t + 1)
                            if t == 0:
                                pe.wait_ge(x_sq, 2)
                        mm = pe.transpose(pt[:, n, T * (k % 2) + P * t:T * (k % 2) + P * (t + 1)],
                                          hreg[t][:, k // 2, P * (k % 2):P * (k % 2 + 1)], ident)
                mm.then_inc(ht_ps, 1)
            pe.wait_ge(w_landed, 16)
            pe.wait_ge(ht_sb, 4)
            for t in range(TT):
                for k in range(KD):
                    mm = pe.matmul(pt[:, 0, E * t:E * (t + 1)], c.hT[:, k, P * t:P * (t + 1)], m.rw[:, k, :], start=k == 0, stop=k == KD - 1)
            mm.then_inc(lg_ps, 1)
            def shared_in(half):
                for j in (2 * half, 2 * half + 1):
                    for k in range(KD):
                        mm = pe.matmul(pt[:, 1 + half, T * (j % 2):T * (j % 2 + 1)], sgw[:, k, P * j:P * (j + 1)], c.hT[:, k, 0:T], start=k == 0, stop=k == KD - 1)
                mm.then_inc(sgu_ps, 1)

            pe.wait_ge(sgw_landed, 32)
            shared_in(0)
            pe.wait_ge(chosen, 1)
            cb = m.rb[:, 0]
            pe.matmul(pt[:, 3, 0:E], m.tub[:], cb[:, 0, :], start=True, stop=True)
            pe.matmul(pt[:, 3, E:2 * E], m.tub[:], cb[:, 1, :], start=True, stop=False)
            pe.matmul(pt[:, 3, E:2 * E], m.oneb[:], cb[:, 0, :], start=False, stop=True)
            for t in range(TT):
                mm = pe.matmul(pt[0:E, 3, 2 * E:2 * E + 1], cb[:, t, :], m.oneb[:, 0:1], start=t == 0, stop=t == TT - 1)
            mm.then_inc(cum_ps, 1)
            shared_in(1)
            pe.wait_ge(parts, 1)
            turned = pt[0:E, 0, :].bitcast(BF16)
            for n in range(4):
                for t in range(TT):
                    pe.transpose(turned[:, P * (2 * n + t):P * (2 * n + t + 1)], m.rb[:, 1 + n, t, :], m.idb[:])
            pe.matmul(pt[0:E, 3, 130:131], m.tub[0:E, 0:E], m.nbb[:], start=True, stop=True).then_inc(tr_ps, 1)
            def shared_out(t):
                for h in range(2):
                    for j in range(2):
                        mm = pe.matmul(pa[:, 2 * t + h, :], m.actT[:, j, P * t:P * (t + 1)], sdw[:, j, 512 * h:512 * (h + 1)], start=j == 0, stop=False, skip_group_check=True)
                mm.then_inc(shared_done, 1)

            pe.wait_ge(sact_ready, 1)
            shared_out(0)
            pe.wait_ge(tr_sb, 1)
            pe.wait_ge(oh_ready, 1)
            for t in range(TT):
                pe.matmul(pt[:, 1, NB * t:NB * (t + 1)], m.trb[:, t, :], m.oh[:], start=True, stop=False, skip_group_check=True)
                pe.matmul(pt[:, 1, NB * t + E:NB * (t + 1)], m.negb[:], m.jm[:], start=False, stop=True, skip_group_check=True)
            for n in range(3):
                for t in range(TT):
                    pe.matmul(pt[:, 2, NB * n:NB * (n + 1)] if t == 0 else pt[:, 0, NB * n:NB * (n + 1)], m.trb[:, 2 + 2 * n + t, :], m.oh[:], start=True, stop=True)
            pe.matmul(pt[0:1, 3, 140:140 + NOV], m.pixb[0:E, :], m.oh[:, E:NB], start=True, stop=True)
            pe.matmul(pt[0:1, 3, 140 + NOV:141 + NOV], m.nbb[:], m.oneb[0:E, 0:1], start=True, stop=True).then_inc(tab_ps, 1)
            shared_out(1)

        @block.scalar
        def _(act):
            ch = Chain(act, r_act)
            for t in range(TT):
                signal(act, act.activation(pt[:, 2 * t:2 * t + 2, :].rearrange("p b n -> p (b n)"), y(t), ACT.Square, accum_out=m.nrm[:, t:t + 1]), y_sq, t + 1)
            act.wait_ge(y_ms, 1)
            signal(act, act.activation(m.nrm[:, 4:6], m.nrm[:, 2:4], ACT.Sqrt), y_rt, 1)
            for t in range(TT):
                act.wait_ge(x_new, t + 1)
                signal(act, act.activation(pt[:, 2 * t:2 * t + 2, :].rearrange("p b n -> p (b n)"), c.x[:, t, :], ACT.Square, accum_out=m.nrm[:, 8 + t:9 + t]), x_sq, t + 1)
            act.wait_ge(x_ms, 1)
            signal(act, act.activation(m.nrm[:, 12:14], m.nrm[:, 10:12], ACT.Sqrt), x_rt, 1)
            for t in range(TT):
                act.wait_ge(h_ready, t + 1)
                signal(act, act.copy(as4(m.hr[:, 0, t, :]), hreg[t]), h_hi, t + 1)
            for n in range(4):
                act.wait_ge(ht_ps, n + 1)
                signal(act, act.copy(c.hT[:, 2 * n:2 * n + 2, 0:T], pt[:, n, :].rearrange("p (k n) -> p k n", k=2)), ht_sb, n + 1)
            act.wait_ge(lg_ps, 1)
            signal(act, act.activation(sc, pt[:, 0, 0:2 * E], ACT.Sigmoid), scores, 1)
            act.wait_ge(sgu_ps, 1)
            signal(act, act.activation(m.sg[:], pt[:, 1, :], ACT.Silu), sgu_act, 1)
            act.wait_ge(tr_ps, 1)
            signal(act, act.copy(m.trb[:].rearrange("p n t -> p (n t)"), pt[0:E, 0, :].bitcast(BF16)), tr_sb, 1)

        @block.vector
        def _(dve):
            ch = Chain(dve, r_dve)
            for out, src in ((m.idb, C_ID), (m.tub, C_TU), (m.oneb, C_ONE)):
                ch.post(dve.tensor_copy(out[:], c.cst[:, src:src + P]))
            ch.post(dve.tensor_copy(m.pixb[:], c.cst[:, C_PIX:C_PIX + 1]))
            ch.post(dve.memset(m.negb[:], -float(CAP)))
            ch.post(dve.tensor_copy(m.oh[:, 0:E], c.cst[0:E, C_ID:C_ID + E]))
            ch.post(dve.tensor_copy(m.tab[:, 0:E], c.cst[0:1, C_IE:C_IE + E]))
            ch.link(dve.memset(m.st[:].bitcast(F32), 0.0))
            dve.wait_ge(y_sq, 2)
            signal(dve, dve.tensor_scalar(m.nrm[:, 2:4], m.nrm[:, 0:2], 1.0 / D, EPS, ALU.mult, ALU.add), y_ms, 1)
            dve.wait_ge(y_rt, 1)
            ch.link(dve.reciprocal(m.nrm[:, 6:8], m.nrm[:, 4:6]))
            dve.wait_ge(m.bc_landed, 48)
            for t in range(TT):
                ch.link(dve.scalar_tensor_tensor(out=hreg[t], in0=as4(y(t)), scalar=m.nrm[:, 6 + t:7 + t], in1=as4(m.bc[:, 0, :]), op0=ALU.mult, op1=ALU.mult))
                signal(dve, dve.tensor_tensor(as4(c.x[:, t, :]), as4(c.x[:, t, :]), hreg[t], ALU.add), x_new, t + 1)
            dve.wait_ge(x_sq, 2)
            signal(dve, dve.tensor_scalar(m.nrm[:, 10:12], m.nrm[:, 8:10], 1.0 / D, EPS, ALU.mult, ALU.add), x_ms, 1)
            dve.wait_ge(x_rt, 1)
            ch.link(dve.reciprocal(m.nrm[:, 14:16], m.nrm[:, 12:14]))
            for t in range(TT):
                ch.link(dve.scalar_tensor_tensor(out=hreg[t], in0=as4(c.x[:, t, :]), scalar=m.nrm[:, 14 + t:15 + t], in1=as4(m.bc[:, 1, :]), op0=ALU.mult, op1=ALU.mult))
                signal(dve, dve.tensor_tensor(hreg[t], hreg[t], as4(m.bc[:, 2, :]), ALU.add), h_ready, t + 1)
            for t in range(TT):
                dve.wait_ge(h_hi, t + 1)
                signal(dve, dve.tensor_tensor(as4(m.hr[:, 1, t, :]), hreg[t], as4(m.hr[:, 0, t, :].bitcast(F32)), ALU.subtract), h_lo, t + 1)
            dve.wait_ge(scores, 1)
            rb = c.rows[:, R_RB + E * layer:R_RB + E * (layer + 1)].unsqueeze(1).broadcast_to([P, TT, E])
            ch.link(dve.tensor_tensor(per_t(sel), per_t(sc), rb, ALU.add))
            for n in range(2 * G):
                ins = dve.max(m8[:, 8 * n:8 * n + 8], sel[:, 8 * n:8 * n + 8])
                ch.post(ins) if n < 2 * G - 1 else ch.link(ins)
            best = m8.rearrange("p (n j) -> p n j", j=8)
            gs = msel[:, 0:16]
            ch.link(dve.tensor_tensor(gs.unsqueeze(2), best[:, :, 0:1], best[:, :, 1:2], ALU.add))
            gst = gs.rearrange("p (t g) -> p t g", t=TT)
            other, own = gst.unsqueeze(2).broadcast_to([P, TT, 8, 8]), gst.unsqueeze(3).broadcast_to([P, TT, 8, 8])
            four = lambda ap: ap.rearrange("p (t g j) -> p t g j", t=TT, g=8)
            before = c.cst[:, C_LT8:C_LT8 + 64].rearrange("p (g j) -> p g j", g=8).unsqueeze(1).broadcast_to([P, TT, 8, 8])
            ch.post(dve.tensor_tensor(four(cmp), other, own, ALU.is_gt))
            ch.link(dve.tensor_tensor(four(cmp2), other, own, ALU.is_equal))
            ch.link(dve.tensor_tensor(four(cmp2), four(cmp2), before, ALU.mult))
            ch.link(dve.tensor_tensor(cmp, cmp, cmp2, ALU.add))
            ch.link(dve.tensor_reduce(rep[:, 0:16], cmp.rearrange("p (n j) -> p n j", j=8), AX.X, ALU.add))
            ch.link(dve.tensor_scalar(rep[:, 16:32], rep[:, 0:16], 3.5, None, ALU.is_lt))
            ch.link(dve.tensor_scalar(rep[:, 32:48], rep[:, 16:32], 1.0, BIG, ALU.subtract, ALU.mult))
            eight = lambda ap: ap.rearrange("p (n j) -> p n j", j=8)
            over8 = lambda ap: ap.unsqueeze(2).broadcast_to([P, 16, 8])
            ch.link(dve.tensor_tensor(eight(msel), eight(sel), over8(rep[:, 16:32]), ALU.mult))
            ch.link(dve.tensor_tensor(eight(msel), eight(msel), over8(rep[:, 32:48]), ALU.add))
            for t in range(TT):
                ch.link(dve.max(m8[:, 8 * t:8 * t + 8], msel[:, E * t:E * (t + 1)]))
            for t in range(TT):
                ch.link(dve.match_replace(rep[:, E * t:E * (t + 1)], m8[:, 8 * t:8 * t + 8], msel[:, E * t:E * (t + 1)], -3e38))
            ch.link(dve.tensor_scalar(sm, rep, -2.0 * BIG, None, ALU.is_lt))
            signal(dve, dve.tensor_copy(m.rb[:, 0], per_t(sm)), chosen, 1)
            ch.link(dve.tensor_tensor(w, sc, sm, ALU.mult))
            ch.link(dve.tensor_reduce(m.nrm[:, 0:2], per_t(w), AX.X, ALU.add))
            ch.link(dve.reciprocal(m.nrm[:, 2:4], m.nrm[:, 0:2]))
            for t in range(TT):
                ch.link(dve.tensor_scalar(w[:, E * t:E * (t + 1)], w[:, E * t:E * (t + 1)], m.nrm[:, 2 + t:3 + t], 2.5, ALU.mult, ALU.mult))
            for n in range(2):
                ch.link(dve.tensor_copy(m.rb[:, 2 + n], per_t(w)))
                ch.link(dve.tensor_tensor(per_t(w), per_t(w), m.rb[:, 2 + n], ALU.subtract))
            ch.link(dve.tensor_copy(m.rb[:, 4], per_t(w)))
            dve.wait_ge(cum_ps, 1)
            ch.link(dve.tensor_tensor(m.rb[:, 1], per_t(pt[:, 3, 0:2 * E]), per_t(sm), ALU.mult))
            cnt = pt[0:E, 3, 2 * E:2 * E + 1]
            ch.link(dve.tensor_copy(m.col[:, 0:1], cnt))
            ch.link(dve.tensor_scalar(m.col[:, 1:2], m.col[:, 0:1], float(CAP), None, ALU.is_gt))
            for n in (2, 3):
                ch.link(dve.scalar_tensor_tensor(out=m.col[:, n:n + 1], in0=m.col[:, 0:1], scalar=float(n * CAP), in1=m.col[:, n - 1:n], op0=ALU.is_gt, op1=ALU.add))
            signal(dve, dve.tensor_copy(m.nbb[:], m.col[:, 3:4]), parts, 1)
            dve.wait_ge(sgu_act, 1)
            dve.wait_ge(sgu_ps, 2)
            signal(dve, dve.tensor_tensor(m.actT[:].rearrange("p j t -> p (j t)"), pt[:, 2, :], m.sg[:], ALU.mult), sact_ready, 1)
            dve.wait_ge(tr_ps, 1)
            ch.link(dve.tensor_copy(m.col[:, 4:5], pt[0:E, 3, 130:131]))
            ch.link(dve.tensor_tensor(m.col[:, 5:6], m.col[:, 4:5], m.col[:, 3:4], ALU.subtract))
            iov = c.cst[0:E, C_IOV:C_IOV + NOV]
            ch.post(dve.tensor_scalar(m.ov[:, 0, :], iov, m.col[:, 5:6], None, ALU.is_ge))
            ch.link(dve.tensor_scalar(m.ov[:, 1, :], iov, m.col[:, 4:5], None, ALU.is_ge))
            ch.link(dve.tensor_tensor(m.ov[:, 0, :], m.ov[:, 0, :], m.ov[:, 1, :], ALU.subtract))
            ch.link(dve.tensor_copy(m.oh[:, E:NB], m.ov[:, 0, :]))
            ch.link(dve.tensor_scalar(m.ov[:, 2, :], iov, m.col[:, 5:6], 1.0, ALU.subtract, ALU.add))
            signal(dve, dve.tensor_tensor(m.jm[:], m.ov[:, 0, :], m.ov[:, 2, :], ALU.mult), oh_ready, 1)
            dve.wait_ge(tab_ps, 1)
            for t in range(TT):
                ch.post(dve.tensor_scalar(m.rk[:, :, t, :], pt[:, 1, NB * t:NB * (t + 1)].rearrange("p (n b) -> p n b", b=2), 1.0, None, ALU.subtract))
                for n in range(3):
                    ch.post(dve.tensor_copy(m.wb[:, :, t, n, :], pt[:, 2 if t == 0 else 0, NB * n:NB * (n + 1)].rearrange("p (n b) -> p n b", b=2)))
            ch.link(dve.tensor_copy(m.tab[:, E:NB + 1], pt[0:1, 3, 140:141 + NOV]))


def own_place(dve, c, m, out, pair):
    places = c.cst[:, C_I64:C_I64 + CAP].unsqueeze(1).broadcast_to([P, 2 * TT, CAP])
    rank = m.rk[:, ds(pair, 1), :, :].rearrange("p n t b -> p (n t b)").unsqueeze(2).broadcast_to([P, 2 * TT, CAP])
    return dve.tensor_tensor(out[:].rearrange("p t (b s) -> p (t b) s", b=2), places, rank, ALU.is_equal)


def experts(nc, c, a, m, layer):
    pt, pa = c.pt, c.pa
    L = str(layer)
    sem = lambda n: c.sem(n + L)
    s_ready, sb_ready = sem("s_ready"), sem("sb_ready")
    x_ps, x_sb, xt_ps, xt_act, xt_dve = (sem(n) for n in ("x_ps", "x_sb", "ext_ps", "ext_act", "ext_dve"))
    gu_ps, silu_done, slot_ps, wsl_ready, st_sb, act_ready = (sem(n) for n in ("gu_ps", "silu_done", "slot_ps", "wsl_ready", "st_sb", "act_ready"))
    at_ps, at_sb, y_ps, y_hi, y_lo, scat = (sem(n) for n in ("at_ps", "at_sb", "ey_ps", "y_hi", "y_lo", "scat"))
    e_dve = sem("e_dve")
    ident = c.cst[:, C_ID:C_ID + P]
    X = m.work[:, 0:D]
    XT = m.work[:, D:2 * D].rearrange("p (k s) -> p k s", k=KD)
    scaled = m.actT[:, :, 0:P]

    def over_pairs(eng, first, body):
        more = further(eng)
        twos = E // 4 + more // 2
        with eng.Fori(first, twos) as i:
            for slot in range(2):
                body(2 * i + slot, slot, i, False)
        with eng.If(more % 2):
            body(2 * twos, 0, twos, True)

    def further(eng):
        return (eng.value_load(m.tab[0:1, NB:NB + 1], min_val=0, max_val=31) + 1) // 2

    with nc.Block() as block:
        @block.sync
        def _(sp):
            sp.dma_start(m.bc[:, 0, :], bc_row(a, (3, 9)[layer])).then_inc(m.bc_landed, 16)

            def body(pair, slot, i, last):
                e = [sp.value_load(m.tab[0:1, ds(2 * pair + ab, 1)], min_val=0, max_val=E - 1) for ab in range(2)]
                for half in range(2):
                    sp.wait_ge(gu_ps, 2 * pair - 3 + half)
                    for ab in range(2):
                        load_gate_up(sp, c, a, m, layer, slot, ab, e[ab], half)
                sp.wait_ge(y_ps, 2 * (pair - 1))
                for ab in range(2):
                    load_down(sp, c, a, m, layer, slot, ab, e[ab])

            over_pairs(sp, 1, body)

        @block.tensor
        def _(pe):
            def gather(pair):
                pe.wait_ge(s_ready, pair + 1)
                for h in range(2):
                    for part in range(2):
                        for t in range(TT):
                            mm = pe.matmul(pt[:, 1 + h, :], m.sr[:, t, :], m.hr[:, part, t, 512 * h:512 * (h + 1)],
                                           start=part + t == 0, stop=part + t == 2)
                    mm.then_inc(x_ps, 1)

            def turn(pair):
                pe.wait_ge(x_sb, 2 * pair + 2)
                for k in range(KD):
                    mm = pe.transpose(pt[:, 1 + k // 4, P * (k % 4):P * (k % 4 + 1)], X[:, P * k:P * (k + 1)], ident)
                    if k % 4 == 3:
                        mm.then_inc(xt_ps, 1)

            def scatter(pair):
                pe.wait_ge(y_lo, 2 * pair + 2)
                for t in range(TT):
                    for h in range(2):
                        for part in range(2):
                            mm = pe.matmul(pa[:, 2 * t + h, :], m.st[:, P * t:P * (t + 1)], m.ys[:, part, 512 * h:512 * (h + 1)],
                                           start=False, stop=False, skip_group_check=True)
                mm.then_inc(scat, 1)

            def body(pair, slot, i, last):
                pe.wait_ge(xt_act, pair + 1)
                pe.wait_ge(xt_dve, pair + 1)
                for k in range(KD):
                    for ab in range(2):
                        if k % 4 == 0:
                            pe.wait_ge(m.gu_landed[slot][ab][k // 4], 16 * i + 16)
                        at = GU_PAIR * slot + GU_PAIR // 2 * ab + 512 * k
                        mm = pe.matmul(pt[CAP * ab:CAP * (ab + 1), 0, :], XT[:, k, CAP * ab:CAP * (ab + 1)], c.gu[:, at:at + 512],
                                       start=k == 0, stop=k == KD - 1)
                    if k % 4 == 3:
                        mm.then_inc(gu_ps, 1)
                scatter(pair)
                pe.wait_ge(sb_ready, pair + 1)
                for t in range(TT):
                    pe.matmul(pt[:, 3, T:T + 6], m.sb[:, t, :], m.wb[:, ds(pair, 1), t, :, :].rearrange("p n a b -> p (n a b)"), start=t == 0, stop=t == TT - 1)
                st = pt[:, 3, 0:P].bitcast(BF16)
                for t in range(TT):
                    mm = pe.transpose(st[:, P * t:P * (t + 1)], m.sb[:, t, :], m.idb[:])
                mm.then_inc(slot_ps, 1)
                gather(pair + 1)
                pe.wait_ge(st_sb, pair + 1)
                pe.wait_ge(act_ready, pair + 1)
                for j in range(2):
                    mm = pe.transpose(pt[:, 3, P * j:P * (j + 1)], m.act[:, P * j:P * (j + 1)], ident)
                mm.then_inc(at_ps, 1)
                turn(pair + 1)
                pe.wait_ge(at_sb, pair + 1)
                for ab in range(2):
                    pe.wait_ge(m.dn_landed[slot][ab], 16 * i + 16)
                for h in range(2):
                    if h == 1:
                        pe.wait_ge(xt_dve, pair + 2)
                    for j in range(2):
                        for ab in range(2):
                            at = DN_PAIR * slot + DN_PAIR // 2 * ab + D * j + 512 * h
                            mm = pe.matmul(pt[CAP * ab:CAP * (ab + 1), 3 - h, :], scaled[:, j, CAP * ab:CAP * (ab + 1)], c.dn[:, at:at + 512],
                                           start=j == 0, stop=j == 1)
                    mm.then_inc(y_ps, 1)

            gather(0)
            turn(0)
            over_pairs(pe, 0, body)
            scatter(E // 2 + further(pe))

        @block.scalar
        def _(act):
            def take(pair):
                for h in range(2):
                    act.wait_ge(x_ps, 2 * pair + h + 1)
                    signal(act, act.copy(X[:, 512 * h:512 * (h + 1)], pt[:, 1 + h, :]), x_sb, 2 * pair + h + 1)

            def take_turned(pair):
                act.wait_ge(xt_ps, 2 * pair + 1)
                signal(act, act.copy(XT[:, 0:4, :].rearrange("p k s -> p (k s)"), pt[:, 1, :]), xt_act, pair + 1)

            def body(pair, slot, i, last):
                act.wait_ge(gu_ps, 2 * pair + 2)
                signal(act, act.activation(m.sg[:, 0:F], pt[:, 0, 0:F], ACT.Silu), silu_done, pair + 1)
                take(pair + 1)
                act.wait_ge(at_ps, pair + 1)
                signal(act, act.copy(scaled, pt[:, 3, 0:T].rearrange("p (j s) -> p j s", j=2)), at_sb, pair + 1)
                take_turned(pair + 1)
                for h in range(2):
                    act.wait_ge(y_ps, 2 * pair + h + 1)
                    act.copy(m.ys[:, 0, 512 * h:512 * (h + 1)], pt[:, 3 - h, :]).then_inc(y_hi, 1)
                if not last:
                    act.wait_ge(y_hi, 2 * pair + 2)

            take(0)
            take_turned(0)
            over_pairs(act, 0, body)

        @block.vector
        def _(dve):
            ch = Chain(dve, e_dve)

            def take_turned(pair):
                dve.wait_ge(xt_ps, 2 * pair + 2)
                signal(dve, dve.tensor_copy(XT[:, 4:8, :].rearrange("p k s -> p (k s)"), pt[:, 2, :]), xt_dve, pair + 1)

            def body(pair, slot, i, last):
                ch.at(2 * pair)
                dve.wait_ge(x_ps, 2 * pair + 2)
                signal(dve, own_place(dve, c, m, m.sr, pair + 1), s_ready, pair + 2)
                dve.wait_ge(slot_ps, pair + 1)
                parts = pt[:, 3, T:T + 6].rearrange("p (n b) -> p b n", b=2)
                for ab in range(2):
                    half = slice(CAP * ab, CAP * (ab + 1))
                    ins = dve.tensor_reduce(m.wsl[half, :], parts[half, ab, :], AX.X, ALU.add)
                    ch.post(ins) if ab == 0 else ch.link(ins)
                signal(dve, dve.tensor_copy(m.st[:], pt[:, 3, 0:P].bitcast(BF16)), st_sb, pair + 1)
                dve.wait_ge(silu_done, pair + 1)
                signal(dve, dve.scalar_tensor_tensor(out=m.act[:], in0=pt[:, 0, F:2 * F], scalar=m.wsl[:], in1=m.sg[:, 0:F], op0=ALU.mult, op1=ALU.mult), act_ready, pair + 1)
                signal(dve, own_place(dve, c, m, m.sb, pair + 1), sb_ready, pair + 2)
                take_turned(pair + 1)
                for h in range(2):
                    dve.wait_ge(y_hi, 2 * pair + h + 1)
                    cols = slice(512 * h, 512 * (h + 1))
                    dve.tensor_tensor(m.ys[:, 1, cols], pt[:, 3 - h, :], m.ys[:, 0, cols].bitcast(F32), ALU.subtract).then_inc(y_lo, 1)
                if not last:
                    dve.wait_ge(y_lo, 2 * pair + 4)

            signal(dve, own_place(dve, c, m, m.sr, 0), s_ready, 1)
            for part in range(2):
                signal(dve, dve.memset(m.ys[:, part, :].bitcast(F32), 0.0), y_lo, part + 1)
            signal(dve, own_place(dve, c, m, m.sb, 0), sb_ready, 1)
            take_turned(0)
            over_pairs(dve, 0, body)


def ffn_end(nc, c, a, m, layer):
    pt, pa = c.pt, c.pa
    L = str(layer)
    f_sq, f_ms, f_rt, f_x, out_done = (c.sem(n + L) for n in ("f_sq", "f_ms", "f_rt", "f_x", "out_done"))
    f_dve = c.sem("f_dve" + L)
    flat = lambda t: pa[:, 2 * t:2 * t + 2, :].rearrange("p b n -> p (b n)")
    with nc.Block() as block:
        @block.scalar
        def _(act):
            for t in range(TT):
                signal(act, act.activation(pt[:, 2 * t:2 * t + 2, :].rearrange("p b n -> p (b n)"), flat(t), ACT.Square, accum_out=m.nrm[:, t:t + 1]), f_sq, t + 1)
            act.wait_ge(f_ms, 1)
            signal(act, act.activation(m.nrm[:, 4:6], m.nrm[:, 2:4], ACT.Sqrt), f_rt, 1)

        @block.vector
        def _(dve):
            ch = Chain(dve, f_dve)
            dve.wait_ge(f_sq, 2)
            signal(dve, dve.tensor_scalar(m.nrm[:, 2:4], m.nrm[:, 0:2], 1.0 / D, EPS, ALU.mult, ALU.add), f_ms, 1)
            dve.wait_ge(f_rt, 1)
            ch.link(dve.reciprocal(m.nrm[:, 6:8], m.nrm[:, 4:6]))
            dve.wait_ge(m.bc_landed, 64)
            for t in range(TT):
                ch.link(dve.scalar_tensor_tensor(out=m.work[:, 0:D], in0=flat(t), scalar=m.nrm[:, 6 + t:7 + t], in1=m.bc[:, 0, :], op0=ALU.mult, op1=ALU.mult))
                signal(dve, dve.tensor_tensor(c.x[:, t, :], c.x[:, t, :], m.work[:, 0:D], ALU.add), f_x, t + 1)

        if layer == 1:
            @block.sync
            def _(sp):
                for t in range(TT):
                    sp.wait_ge(f_x, t + 1)
                    sp.dma_start(a["out"][t], c.x[:, t, :]).then_inc(out_done, 16)
                sp.wait_ge(out_done, 32)



def conformer(nc, c, a, s):
    pt, pa = c.pt, c.pa
    xn = c.sb("cxn", [P, TT, D], F32, s)
    u = c.sb("cu", [P, KD, NROW, PADROW], F32, s)
    v = c.sb("cvs", [P, KD, T], F32, s)
    sq = c.sb("csq", [P, KD, T], F32, s)
    rstd = c.sb("crstd", [P, T], F32, s)
    nrm = c.sb("cnrm", [P, 8], F32, s)
    in_landed = [c.sem(f"cvin_landed{j}") for j in range(KD)]
    out_landed = c.sem("cvout_landed")
    x_sq, x_ms, x_rt, xn_ready, xt_ps, h_sb = (c.sem(n) for n in ("cx_sq", "cx_ms", "cx_rt", "cxn_ready", "cxt_ps", "ch_sb"))
    glu_ps, gate_done, u_ready, v_ready, mu_ps, xc_ready, sq_ready, var_ps, var_e, std, ln_ready, sw, co_ps = (
        c.sem(n) for n in ("glu_ps", "gate_done", "u_ready", "v_ready", "mu_ps", "xc_ready", "sq_ready", "var_ps", "var_e", "std", "ln_ready", "swish", "co_ps"))
    c_dve, padded = c.sem("c_dve"), c.sem("padded")
    SPLIT, OWN, SHARED, DIAG, HANDOVER = (1, 4), (0, 2, 3, 5), 6, 7, 13
    FINISHED = OWN + (SHARED, DIAG)
    diag = c.sb("cdiag", [P, TAP31, P], F32, s)
    diag_ready, diag_ps = c.sem("diag_ready"), c.sem("diag_ps")
    product, summed = c.sem("product"), c.sem("summed")
    prod = c.sb("cprod", [P, 4, T], F32, s)
    sigm = sq
    ident = c.cst[:, C_ID:C_ID + P]
    ones = c.cst[:, C_ONE:C_ONE + P]
    shift = c.adac[:, 4 * KD:5 * KD]
    scale = c.adac[:, 5 * KD:6 * KD]
    win = [c.gu[:, 2048 * j:2048 * (j + 1)].rearrange("p (k n) -> p k n", k=KD) for j in range(KD)]
    wout = c.dn[:].rearrange("p (k n) -> p k n", k=KD)
    pair = lambda n: pt[:, 2 * n:2 * n + 2, :].rearrange("p b n -> p (b n)")
    rows = lambda ap: ap.rearrange("p (r l) -> p r l", r=NROW)

    def conv_tap(dve, j, tap):
        w = c.vec[:, V_DW + TAP31 * j + tap:V_DW + TAP31 * j + tap + 1]
        src = u[:, j, :, tap:tap + ROW]
        if tap == 0:
            return dve.tensor_scalar(rows(v[:, j, :]), src, w, c.vec[:, V_DWB + j:V_DWB + j + 1], ALU.mult, ALU.add)
        return dve.scalar_tensor_tensor(out=rows(v[:, j, :]), in0=src, scalar=w, in1=rows(v[:, j, :]), op0=ALU.mult, op1=ALU.add)

    with nc.Block() as block:
        @block.gpsimd
        def _(pool):
            signal(pool, pool.memset(u[:], 0.0), padded, 1)
            for n, j in enumerate(SPLIT + (SHARED,)):
                for tap in range(1, HANDOVER if j == SHARED else TAP31):
                    pool.wait_ge(product, TAP31 * n + tap + 1)
                    signal(pool, pool.tensor_tensor(v[:, j, :], v[:, j, :], prod[:, tap % 4, :], ALU.add), summed, (TAP31 - 1) * n + tap)

        @block.sync
        def _(sp):
            for j in range(KD):
                sp.dma_start(c.gu[:, 2048 * j:2048 * (j + 1)], a["cv_in"][j]).then_inc(in_landed[j], 16)
            sp.dma_start(c.dn[:], a["cv_out"]).then_inc(out_landed, 16)

        @block.tensor
        def _(pe):
            pe.wait_ge(x_sq, 2)
            for n in range(4):
                for k in (2 * n, 2 * n + 1):
                    for t in range(TT):
                        if n == 0:
                            pe.wait_ge(xn_ready, t + 1)
                        mm = pe.transpose(pt[:, n, T * (k % 2) + P * t:T * (k % 2) + P * (t + 1)], xn[:, t, P * k:P * (k + 1)], ident)
                mm.then_inc(xt_ps, 1)
            pe.wait_ge(h_sb, KD)
            for j in range(KD):
                pe.wait_ge(in_landed[j], 16)
                if j >= 2:
                    pe.wait_ge(u_ready, j - 1)
                for half in range(2):
                    for k in range(KD):
                        mm = pe.matmul(pt[:, 2 * (j % 2) + half, 0:T], win[j][:, k, P * half:P * (half + 1)], c.hT[:, k, 0:T], start=k == 0, stop=k == KD - 1)
                mm.then_inc(glu_ps, 1)
            pe.wait_ge(diag_ready, TAP31)
            pe.wait_ge(u_ready, DIAG + 1)
            for tap in range(TAP31):
                mm = pe.matmul(pt[:, 0, 0:T], diag[:, tap, :], u[:, DIAG, :, tap:tap + ROW], start=tap == 0, stop=tap == TAP31 - 1)
            mm.then_inc(diag_ps, 1)
            order = sorted(OWN + SPLIT) + [SHARED, DIAG]
            for k in order:
                if k in SPLIT:
                    pe.wait_ge(summed, (TAP31 - 1) * (SPLIT.index(k) + 1))
                else:
                    pe.wait_ge(v_ready, FINISHED.index(k) + 1)
                mm = pe.matmul(pa[:, 0, 0:T], ones, v[:, k, :], start=k == order[0], stop=k == order[-1])
            mm.then_inc(mu_ps, 1)
            for k in range(KD):
                pe.wait_ge(sq_ready, k + 1)
                mm = pe.matmul(pa[:, 1, 0:T], ones, sq[:, k, :], start=k == 0, stop=k == KD - 1)
            mm.then_inc(var_ps, 1)
            pe.wait_ge(var_e, 1)
            for t in range(TT):
                for h in range(2):
                    pe.matmul(pa[:, 2 * t + h, :], ones[0:1, :], c.rows[0:1, R_BO + 512 * h:R_BO + 512 * (h + 1)], start=True, stop=False, skip_group_check=True)
            pe.wait_ge(out_landed, 16)
            for k in range(KD):
                pe.wait_ge(sw, k + 1)
                for t in range(TT):
                    for h in range(2):
                        mm = pe.matmul(pa[:, 2 * t + h, :], v[:, k, P * t:P * (t + 1)], wout[:, k, 512 * h:512 * (h + 1)], start=False, stop=k == KD - 1, skip_group_check=True)
            mm.then_inc(co_ps, 1)

        @block.scalar
        def _(act):
            for t in range(TT):
                signal(act, act.activation(pair(t), c.x[:, t, :], ACT.Square, accum_out=nrm[:, t:t + 1]), x_sq, t + 1)
            act.wait_ge(x_ms, 1)
            signal(act, act.activation(nrm[:, 4:6], nrm[:, 2:4], ACT.Sqrt), x_rt, 1)
            for k in range(KD):
                act.wait_ge(xt_ps, k // 2 + 1)
                signal(act, act.activation(c.hT[:, k, 0:T], pt[:, k // 2, T * (k % 2):T * (k % 2 + 1)], ACT.Identity,
                                           bias=shift[:, k:k + 1], scale=scale[:, k:k + 1]), h_sb, k + 1)
            def gate(j):
                act.wait_ge(glu_ps, j + 1)
                signal(act, act.activation(sigm[:, j, :], pt[:, 2 * (j % 2) + 1, 0:T], ACT.Sigmoid, bias=c.vec[:, V_CBI + KD + j:V_CBI + KD + j + 1]), gate_done, j + 1)

            for tap in range(TAP31):
                w = c.vec[:, V_DW + TAP31 * DIAG + tap:V_DW + TAP31 * DIAG + tap + 1]
                act.activation(diag[:, tap, :], ident, ACT.Copy, scale=w).then_inc(diag_ready, 1)
            gate(0)
            gate(1)
            gates = {(n, tap): 2 + 3 * n + i for n in range(2) for i, tap in enumerate(((8, 18, 28), (6, 16, 26))[n])}
            for n, j in enumerate(SPLIT + (SHARED,)):
                act.wait_ge(u_ready, j + 1)
                for tap in range(HANDOVER if j == SHARED else TAP31):
                    if (n, tap) in gates:
                        gate(gates[n, tap])
                    w = c.vec[:, V_DW + TAP31 * j + tap:V_DW + TAP31 * j + tap + 1]
                    if tap == 0:
                        ins = act.activation(rows(v[:, j, :]), u[:, j, :, tap:tap + ROW], ACT.Identity, bias=c.vec[:, V_DWB + j:V_DWB + j + 1], scale=w)
                    else:
                        if (TAP31 - 1) * n + tap > 4:
                            act.wait_ge(summed, (TAP31 - 1) * n + (tap - 4 if tap > 4 else 0))
                        ins = act.activation(rows(prod[:, tap % 4, :]), u[:, j, :, tap:tap + ROW], ACT.Copy, scale=w)
                    ins.then_inc(product, 1)
            act.wait_ge(product, TAP31 * len(SPLIT) + HANDOVER)
            for k in range(KD):
                act.wait_ge(xc_ready, k + 1)
                signal(act, act.activation(sq[:, k, :], v[:, k, :], ACT.Square), sq_ready, k + 1)
            act.wait_ge(var_e, 1)
            signal(act, act.activation(rstd[:], rstd[:], ACT.Sqrt), std, 1)
            for k in range(KD):
                act.wait_ge(ln_ready, k + 1)
                signal(act, act.activation(v[:, k, :], v[:, k, :], ACT.Silu, bias=c.vec[:, V_LNB + k:V_LNB + k + 1], scale=c.vec[:, V_LNG + k:V_LNG + k + 1]), sw, k + 1)

        @block.vector
        def _(dve):
            ch = Chain(dve, c_dve)
            dve.wait_ge(x_sq, 2)
            signal(dve, dve.tensor_scalar(nrm[:, 2:4], nrm[:, 0:2], 1.0 / D, EPS, ALU.mult, ALU.add), x_ms, 1)
            dve.wait_ge(x_rt, 1)
            ch.link(dve.reciprocal(nrm[:, 6:8], nrm[:, 4:6]))
            for t in range(TT):
                signal(dve, dve.tensor_scalar(xn[:, t, :], c.x[:, t, :], nrm[:, 6 + t:7 + t], None, ALU.mult), xn_ready, t + 1)

            def gated(j):
                dve.wait_ge(gate_done, j + 1)
                signal(dve, dve.scalar_tensor_tensor(out=u[:, j, :, TAP31 // 2:TAP31 // 2 + ROW], in0=rows(pt[:, 2 * (j % 2), 0:T]), scalar=c.vec[:, V_CBI + j:V_CBI + j + 1],
                                                     in1=rows(sigm[:, j, :]), op0=ALU.add, op1=ALU.mult), u_ready, j + 1)

            dve.wait_ge(padded, 1)
            gated(0)
            gatings = {(0, 14): 1, (0, 28): 2, (1, 14): 3, (1, 28): 4, (2, 12): 5, (2, 24): 6, (3, 4): 7}
            for n, j in enumerate(OWN):
                for tap in range(TAP31):
                    if (n, tap) in gatings:
                        gated(gatings[n, tap])
                    ins = conv_tap(dve, j, tap)
                    if tap < TAP31 - 1:
                        ch.link(ins)
                signal(dve, ins, v_ready, n + 1)
            dve.wait_ge(summed, (TAP31 - 1) * len(SPLIT) + HANDOVER - 1)
            for tap in range(HANDOVER, TAP31):
                ins = conv_tap(dve, SHARED, tap)
                if tap < TAP31 - 1:
                    ch.link(ins)
            signal(dve, ins, v_ready, len(OWN) + 1)
            dve.wait_ge(diag_ps, 1)
            signal(dve, dve.tensor_scalar(v[:, DIAG, :], pt[:, 0, 0:T], c.vec[:, V_DWB + DIAG:V_DWB + DIAG + 1], None, ALU.add), v_ready, len(OWN) + 2)
            dve.wait_ge(mu_ps, 1)
            ch.link(dve.tensor_scalar(rstd[:], pa[:, 0, 0:T], 1.0 / D, None, ALU.mult))
            for k in range(KD):
                signal(dve, dve.tensor_tensor(v[:, k, :], v[:, k, :], rstd[:], ALU.subtract), xc_ready, k + 1)
            dve.wait_ge(var_ps, 1)
            signal(dve, dve.tensor_scalar(rstd[:], pa[:, 1, 0:T], 1.0 / D, EPS, ALU.mult, ALU.add), var_e, 1)
            dve.wait_ge(std, 1)
            ch.link(dve.reciprocal(rstd[:], rstd[:]))
            for k in range(KD):
                signal(dve, dve.tensor_tensor(v[:, k, :], v[:, k, :], rstd[:], ALU.mult), ln_ready, k + 1)



def constants():
    i = np.arange(P)
    cst = np.zeros((P, C_N), np.float32)
    cst[:, C_ID:C_ID + P] = np.eye(P)
    cst[:, C_TU:C_TU + P] = i[:, None] <= i[None, :]
    cst[:, C_TL:C_TL + P] = i[:, None] >= i[None, :]
    cst[:, C_ONE:C_ONE + P] = 1.0
    cst[:, C_MF:C_MF + P] = np.where(i[:, None] <= i[None, :], 0.0, -BIG)
    cst[:, C_MB:C_MB + P] = np.where(i[:, None] >= i[None, :], 0.0, -BIG)
    cst[:, C_I64:C_I64 + CAP] = np.arange(CAP)
    cst[:, C_IOV:C_IOV + NOV] = np.arange(NOV)
    cst[:, C_LT8:C_LT8 + 64] = (np.arange(8)[None, :] < np.arange(8)[:, None]).reshape(-1)
    cst[:, C_PIX] = i
    cst[:, C_IE:C_IE + E] = np.arange(E)
    return cst


def chunked(v):
    return np.asarray(v).reshape(-1, P).T


def k_major(w):
    k, n = w.shape
    return w.reshape(k // P, P, n).transpose(1, 0, 2).reshape(P, -1)


def layout(i):
    ada_w, ada_b = i["ada_w"], i["ada_b"]
    part = lambda arr, l, n: arr[l][..., n * D:(n + 1) * D]
    order = [(0, 2, i["norm_mix_post"][0], 0), (0, 4, i["norm_ffn_pre"][0], 1), (0, 3, None, 0), (0, 5, i["norm_ffn_post"][0], 0),
             (1, 0, None, 0), (1, 1, i["norm_mix_pre"][1], 1), (1, 2, i["norm_mix_post"][1], 0),
             (1, 4, i["norm_ffn_pre"][1], 1), (1, 3, None, 0), (1, 5, i["norm_ffn_post"][1], 0)]
    rest = np.concatenate([part(ada_w, l, n) for l, n, _, _ in order], axis=1)
    first = np.concatenate([part(ada_w, 0, 0), part(ada_w, 0, 1)], axis=1)
    one = np.ones(D, np.float32)
    vec = np.zeros((P, V_N), np.float32)

    def put(at, v):
        v = chunked(v)
        vec[:, at:at + v.shape[1]] = v

    put(V_NPRE, i["norm_mix_pre"][0])
    put(V_BSH, part(ada_b, 0, 0))
    put(V_BSC, part(ada_b, 0, 1))
    ada_par = np.stack([np.concatenate([part(ada_b, l, n) for l, n, _, _ in order]),
                        np.concatenate([one * o for _, _, _, o in order]),
                        np.concatenate([one if m is None else m for _, _, m, _ in order])])
    cw = np.concatenate([i["ssm_conv_w"][0], i["ssm_conv_b"][0][None]], axis=0).reshape(TAPS + 1, 32, P)
    chunk = [[2 * g, 2 * g + 1, 2 * G + g, 3 * G + g] for g in range(G)]
    vec[:, V_CONV:V_SN] = cw[:, chunk, :].transpose(3, 1, 2, 0).reshape(P, -1)
    put(V_SN, i["ssm_norm"][0])
    put(V_CBI, i["cv_b_in"][0])
    vec[:, V_DW:V_DWB] = i["cv_dw_w"][0].reshape(TAP31, KD, P).transpose(2, 1, 0).reshape(P, -1)
    put(V_DWB, i["cv_dw_b"][0])
    put(V_LNG, i["cv_ln_g"][0])
    put(V_LNB, i["cv_ln_b"][0])
    w = i["ssm_w_in"][0]
    z0, x0, b0, c0, d0 = 0, 2 * D, 4 * D, 4 * D + G * P, 4 * D + 2 * G * P
    w_in = np.stack([k_major(np.concatenate([w[:, x0 + GW * g:x0 + GW * (g + 1)], w[:, b0 + P * g:b0 + P * (g + 1)],
                                             w[:, c0 + P * g:c0 + P * (g + 1)], w[:, z0 + GW * g:z0 + GW * (g + 1)]], axis=1)) for g in range(G)])
    gate_up = np.concatenate([i["exp_w_gate"].reshape(2, E, KD, P, F), i["exp_w_up"].reshape(2, E, KD, P, F)], axis=-1)
    return {
        "x": i["x"].reshape(TT, P, D),
        "ctx": i["ctx"].reshape(TT, P, D),
        "cvec": np.stack([chunked(i["c"][0]), chunked(i["c_ctx"])], axis=2),
        "consts": constants(),
        "vecs": vec,
        "rows": np.concatenate([i["ssm_d"][0], i["router_b"].reshape(-1), i["cv_b_out"][0]]),
        "ada_par": ada_par.reshape(3, 80, P).transpose(1, 0, 2).reshape(80, 3 * P),
        "dtcols": np.stack([i["ssm_dt_bias"][0].reshape(-1), i["ssm_a_log"][0].reshape(-1)], axis=1),
        "ada_first": np.stack([k_major(first[:, 512 * n:512 * (n + 1)]) for n in range(4)]),
        "ada_rest": rest.reshape(KD, P, G, ADA_G).transpose(2, 0, 1, 3).reshape(G * KD, P, ADA_G),
        "w_in": w_in,
        "w_dt": k_major(w[:, d0:]).reshape(P, KD, 64),
        "w_out": i["ssm_w_out"][0].reshape(G, 2, P, D).transpose(0, 2, 1, 3).reshape(G, P, 2 * D),
        "router_w": np.stack([k_major(i["router_w"][l]) for l in range(2)]),
        "gate_up": gate_up.transpose(0, 1, 3, 2, 4).reshape(2 * E, P, KD * 2 * F),
        "down": i["exp_w_down"].reshape(2 * E, 2, P, D).transpose(0, 2, 1, 3).reshape(2 * E, P, 2 * D),
        "sh_gate_up": np.stack([k_major(np.concatenate([i["sh_w_gate"][l], i["sh_w_up"][l]], axis=1)) for l in range(2)]),
        "sh_down": i["sh_w_down"].reshape(2, 2, P, D).transpose(0, 2, 1, 3).reshape(2, P, 2 * D),
        "cv_in": np.stack([k_major(np.concatenate([i["cv_w_in"][0][:, P * j:P * (j + 1)], i["cv_w_in"][0][:, D + P * j:D + P * (j + 1)]], axis=1)) for j in range(KD)]),
        "cv_out": k_major(i["cv_w_out"][0]),
    }


def program(nc, shapes):
    a = {}
    for name, (shape, dt) in shapes.items():
        a[name] = nc.dram_tensor("in_" + name, shape, dt, kind="ExternalInput").ap()
    a["out"] = nc.dram_tensor("out", (TT, P, D), F32, kind="ExternalOutput").ap()
    a["cs_scr"] = nc.dram_tensor("cs_scr", (64, T), F32).ap()
    a["ada_raw"] = nc.dram_tensor("ada_raw", (G, ADA_G), F32).ap()
    a["ada_scr"] = nc.dram_tensor("ada_scr", (80, P), F32).ap()
    build(nc, a)


def kernel(**inputs):
    import concourse.bacc as bacc
    from concourse.bass_utils import run_bass_kernel_spmd

    arrays = {"in_" + n: np.ascontiguousarray(v) for n, v in layout({n: np.asarray(v) for n, v in inputs.items()}).items()}
    nc = bacc.Bacc("TRN2", target_bir_lowering=False, num_devices=1)
    program(nc, {n[3:]: (v.shape, mybir.dt.from_np(v.dtype)) for n, v in arrays.items()})
    r = run_bass_kernel_spmd(nc, [arrays], core_ids=[0])
    return r.results[0]["out"].reshape(1, T, D)
```
